# Optimizing a Trainium2 kernel written in Bass

```python
import jax, jax.numpy as jnp
from jax import lax
import numpy as np

D_MODEL = 2048
BATCH = 1
SEQ = 256
DEPTH = 2
DEC_BATCH = 8
DEC_SEQ = 4
PAST_LEN = 2048
PAGE_SIZE = 128

ATTN_WIDTH = D_MODEL // 2
HG_WIDTH = D_MODEL // 4
CONV_WIDTH = D_MODEL // 4
MIX_WIDTH = ATTN_WIDTH + HG_WIDTH + CONV_WIDTH

HEAD_DIM = 64
N_Q_HEADS = ATTN_WIDTH // HEAD_DIM
N_KV_HEADS = N_Q_HEADS // 4
Q_PER_KV = N_Q_HEADS // N_KV_HEADS
KV_WIDTH = N_KV_HEADS * HEAD_DIM
WINDOW = 128
ROPE_THETA = 500000.0
ROT_DIM = HEAD_DIM // 4
ATTN_SCALE = HEAD_DIM ** -0.5
NEG_BIG = -1e30

HG_DV = 128
HG_HEADS = HG_WIDTH // HG_DV
HG_DK = 128
HG_KEY = HG_HEADS * HG_DK
HG_CHUNK = 64
LB_TINY = 1e-30

CONV_K = 3

D_FF = -(-8 * D_MODEL // (3 * 256)) * 256

NORM_EPS = 1e-6
IN_SIZES = (ATTN_WIDTH, KV_WIDTH, KV_WIDTH,
            HG_KEY, HG_KEY, HG_WIDTH, HG_WIDTH,
            CONV_WIDTH, CONV_WIDTH, CONV_WIDTH)
IN_WIDTH = sum(IN_SIZES)

kernel_name = "hymba_swa_hgrn2_shortconv_decode_step"

def rms_norm(x, g):
    xf = x.astype(jnp.float32)
    y = xf * lax.rsqrt(jnp.mean(xf * xf, axis=-1, keepdims=True) + NORM_EPS)
    return (y * g.astype(jnp.float32)).astype(x.dtype)

def partial_rope(x, pos):
    half = ROT_DIM // 2
    inv = ROPE_THETA ** (-jnp.arange(half, dtype=jnp.float32) * 2.0 / ROT_DIM)
    ang = pos.astype(jnp.float32)[:, None] * inv[None, :]
    cos = jnp.cos(ang)[:, None, :]
    sin = jnp.sin(ang)[:, None, :]
    xr = x[..., :ROT_DIM].astype(jnp.float32)
    x1, x2 = xr[..., :half], xr[..., half:]
    rot = jnp.concatenate([x1 * cos - x2 * sin, x2 * cos + x1 * sin], axis=-1)
    return jnp.concatenate([rot.astype(x.dtype), x[..., ROT_DIM:]], axis=-1)

def sink_attend(q, k, v, mask, sink):
    s = jnp.einsum('bnqhgd,bnshd->bnhgqs', q, k).astype(jnp.float32) * ATTN_SCALE
    s = jnp.where(mask[None, :, None, None], s, NEG_BIG)
    sk = sink.astype(jnp.float32).reshape(N_KV_HEADS, Q_PER_KV)[None, None, :, :, None, None]
    m = jnp.maximum(jnp.max(s, axis=-1, keepdims=True), sk)
    p = jnp.exp(s - m)
    p = p / (jnp.sum(p, axis=-1, keepdims=True) + jnp.exp(sk - m))
    return jnp.einsum('bnhgqs,bnshd->bnqhgd', p.astype(v.dtype), v)

def swa_prompt(q, k, v, sink):
    B, L, _ = q.shape
    C = WINDOW
    N = L // C
    pos = jnp.arange(L, dtype=jnp.int32)
    q = partial_rope(q.reshape(B, L, N_Q_HEADS, HEAD_DIM), pos)
    k = partial_rope(k.reshape(B, L, N_KV_HEADS, HEAD_DIM), pos)
    v = v.reshape(B, L, N_KV_HEADS, HEAD_DIM)
    qb = q.reshape(B, N, C, N_KV_HEADS, Q_PER_KV, HEAD_DIM)
    kb = k.reshape(B, N, C, N_KV_HEADS, HEAD_DIM)
    vb = v.reshape(B, N, C, N_KV_HEADS, HEAD_DIM)
    pad = ((0, 0), (1, 0), (0, 0), (0, 0), (0, 0))
    kk = jnp.concatenate([jnp.pad(kb, pad)[:, :-1], kb], axis=2)
    vv = jnp.concatenate([jnp.pad(vb, pad)[:, :-1], vb], axis=2)
    blk = jnp.arange(N, dtype=jnp.int32)[:, None] * C
    qpos = blk + jnp.arange(C, dtype=jnp.int32)[None, :]
    kpos = blk - C + jnp.arange(2 * C, dtype=jnp.int32)[None, :]
    diff = qpos[:, :, None] - kpos[:, None, :]
    mask = (diff >= 0) & (diff <= WINDOW) & (kpos[:, None, :] >= 0)
    o = sink_attend(qb, kk, vv, mask, sink).reshape(B, L, ATTN_WIDTH)
    keep = min(WINDOW, L)
    return o, k[:, L - keep:], v[:, L - keep:]

def swa_sample(q, k, v, k_buf, v_buf, sink):
    B, L, _ = q.shape
    Lb = k_buf.shape[1]
    pos = PAST_LEN + jnp.arange(L, dtype=jnp.int32)
    q = partial_rope(q.reshape(B, L, N_Q_HEADS, HEAD_DIM), pos)
    k = partial_rope(k.reshape(B, L, N_KV_HEADS, HEAD_DIM), pos)
    v = v.reshape(B, L, N_KV_HEADS, HEAD_DIM)
    kk = jnp.concatenate([k_buf.astype(k.dtype), k], axis=1)
    vv = jnp.concatenate([v_buf.astype(v.dtype), v], axis=1)
    kpos = jnp.concatenate([PAST_LEN - Lb + jnp.arange(Lb, dtype=jnp.int32), pos])
    diff = pos[:, None] - kpos[None, :]
    mask = (diff >= 0) & (diff <= WINDOW)
    qb = q.reshape(B, 1, L, N_KV_HEADS, Q_PER_KV, HEAD_DIM)
    o = sink_attend(qb, kk[:, None], vv[:, None], mask[None], sink).reshape(B, L, ATTN_WIDTH)
    return o, kk[:, -Lb:], vv[:, -Lb:]

def hgrn2_chunked(q, log_f, k, v, S0):
    B, L, H, DK = q.shape
    c = HG_CHUNK if L % HG_CHUNK == 0 else L
    n = L // c

    def chunks(a):
        return jnp.swapaxes(a.reshape(B, n, c, H, a.shape[-1]), 0, 1)

    causal = jnp.tril(jnp.ones((c, c), dtype=bool))[None, :, :, None, None]

    def step(S, inp):
        qc, gc, kc, vc = inp
        G = jnp.cumsum(gc, axis=1)
        G_last = G[:, -1]
        o_inter = jnp.einsum('bthd,bhde->bthe', qc * jnp.exp(G), S)
        decay = jnp.exp(jnp.where(causal, G[:, :, None] - G[:, None, :], NEG_BIG))
        A = jnp.einsum('bthd,btshd->btsh', qc, decay * kc[:, None])
        o_intra = jnp.einsum('btsh,bshe->bthe', A, vc)
        S_new = S * jnp.exp(G_last)[..., None] + jnp.einsum(
            'bshd,bshe->bhde', kc * jnp.exp(G_last[:, None] - G), vc)
        return S_new, o_inter + o_intra

    S_fin, o = lax.scan(step, S0, (chunks(q), chunks(log_f), chunks(k), chunks(v)))
    o = jnp.swapaxes(o, 0, 1).reshape(B, L, H, v.shape[-1])
    return o, S_fin

def hgrn2_mixer(hq, hf, hi, hg, S0, lb, g_norm):
    B, L, _ = hq.shape
    lb = lb.reshape(HG_HEADS, HG_DK)
    q = (jax.nn.silu(hq.astype(jnp.float32)) * HG_DK ** -0.5).reshape(B, L, HG_HEADS, HG_DK)
    fpre = hf.astype(jnp.float32).reshape(B, L, HG_HEADS, HG_DK)
    log_lb = jnp.log(jnp.maximum(lb, LB_TINY))
    log_f = jnp.logaddexp(log_lb, jnp.log1p(-lb) + jax.nn.log_sigmoid(fpre))
    k = (1.0 - lb) * jax.nn.sigmoid(-fpre)
    v = hi.astype(jnp.float32).reshape(B, L, HG_HEADS, HG_DV)
    o, S_fin = hgrn2_chunked(q, log_f, k, v, S0)
    o = rms_norm(o, g_norm).reshape(B, L, HG_WIDTH).astype(hq.dtype)
    return o * jax.nn.silu(hg), S_fin

def short_conv(u, buf, w):
    L = u.shape[1]
    up = jnp.concatenate([buf.astype(u.dtype), u], axis=1)
    y = w[0] * up[:, 0:L]
    for j in range(1, CONV_K):
        y = y + w[j] * up[:, j:j + L]
    return y, up[:, -(CONV_K - 1):]

def run_trunk(x, k_cache, v_cache, s_cache, c_cache, w_in, attn_sink, lower_bound, hgrn_norm,
              conv_w, w_out, norm_mix, norm_ffn, w_gate_up, w_down, norm_final):
    B = x.shape[0]
    sample = k_cache is not None
    split_idx = np.cumsum(IN_SIZES)[:-1].tolist()
    ks, vs, ss, cs = [], [], [], []
    for l in range(DEPTH):
        h = rms_norm(x, norm_mix[l])
        proj = h @ w_in[l]
        q, k, v, hq, hf, hi, hg, cb, cc, ch = jnp.split(proj, split_idx, axis=-1)
        if sample:
            a, k_new, v_new = swa_sample(q, k, v, k_cache[l], v_cache[l], attn_sink[l])
            S0 = s_cache[l].astype(jnp.float32)
            buf = c_cache[l]
        else:
            a, k_new, v_new = swa_prompt(q, k, v, attn_sink[l])
            S0 = jnp.zeros((B, HG_HEADS, HG_DK, HG_DV), jnp.float32)
            buf = jnp.zeros((B, CONV_K - 1, CONV_WIDTH), x.dtype)
        o, S_new = hgrn2_mixer(hq, hf, hi, hg, S0, lower_bound[l], hgrn_norm[l])
        yc, buf_new = short_conv(cc * ch, buf, conv_w[l])
        x = x + jnp.concatenate([a, o, cb * yc], axis=-1) @ w_out[l]
        h = rms_norm(x, norm_ffn[l])
        gate, up = jnp.split(h @ w_gate_up[l], 2, axis=-1)
        x = x + (jax.nn.silu(gate) * up) @ w_down[l]
        ks.append(k_new)
        vs.append(v_new)
        ss.append(S_new.astype(x.dtype))
        cs.append(buf_new)
    y = rms_norm(x, norm_final)
    return y, jnp.stack(ks), jnp.stack(vs), jnp.stack(ss), jnp.stack(cs)

def setup_inputs(seed: int = 0) -> dict:
    key = jax.random.key(seed)
    ks = jax.random.split(key, 17)
    f32 = jnp.float32
    win_buf = min(WINDOW, PAST_LEN)
    nrm = lambda k, shape, s: jax.random.normal(k, shape, f32) * s
    return {
        "x_prompt": nrm(ks[0], (BATCH, SEQ, D_MODEL), 1.0),
        "x_sample": nrm(ks[1], (DEC_BATCH, DEC_SEQ, D_MODEL), 1.0),
        "cache_attn_k": nrm(ks[2], (DEPTH, DEC_BATCH, win_buf, N_KV_HEADS, HEAD_DIM), 1.0),
        "cache_attn_v": nrm(ks[3], (DEPTH, DEC_BATCH, win_buf, N_KV_HEADS, HEAD_DIM), 1.0),
        "state_hgrn": nrm(ks[4], (DEPTH, DEC_BATCH, HG_HEADS, HG_DK, HG_DV), 0.5),
        "state_conv": nrm(ks[5], (DEPTH, DEC_BATCH, CONV_K - 1, CONV_WIDTH), 1.0),
        "w_in": nrm(ks[6], (DEPTH, D_MODEL, IN_WIDTH), D_MODEL ** -0.5),
        "attn_sink": nrm(ks[7], (DEPTH, N_Q_HEADS), 1.0),
        "hgrn_lower_bounds": nrm(ks[8], (DEPTH, HG_KEY), 0.1),
        "hgrn_norm": 1.0 + nrm(ks[9], (DEPTH, HG_HEADS, HG_DV), 0.02),
        "conv_w": nrm(ks[10], (DEPTH, CONV_K, CONV_WIDTH), CONV_K ** -0.5),
        "w_out": nrm(ks[11], (DEPTH, MIX_WIDTH, D_MODEL), MIX_WIDTH ** -0.5),
        "norm_mix": 1.0 + nrm(ks[12], (DEPTH, D_MODEL), 0.02),
        "norm_ffn": 1.0 + nrm(ks[13], (DEPTH, D_MODEL), 0.02),
        "w_gate_up": nrm(ks[14], (DEPTH, D_MODEL, 2 * D_FF), D_MODEL ** -0.5),
        "w_down": nrm(ks[15], (DEPTH, D_FF, D_MODEL), D_FF ** -0.5),
        "norm_final": 1.0 + nrm(ks[16], (D_MODEL,), 0.02),
    }

def reference(x_prompt, x_sample, cache_attn_k, cache_attn_v, state_hgrn, state_conv,
              w_in, attn_sink, hgrn_lower_bounds, hgrn_norm, conv_w, w_out,
              norm_mix, norm_ffn, w_gate_up, w_down, norm_final):
    lbp = jax.nn.softmax(hgrn_lower_bounds.astype(jnp.float32), axis=0)
    lower_bound = jnp.cumsum(lbp, axis=0) - lbp[0:1]
    y_prompt, k_p, v_p, s_p, c_p = run_trunk(
        x_prompt, None, None, None, None, w_in, attn_sink, lower_bound, hgrn_norm,
        conv_w, w_out, norm_mix, norm_ffn, w_gate_up, w_down, norm_final)
    y_sample, k_s, v_s, s_s, c_s = run_trunk(
        x_sample, cache_attn_k, cache_attn_v, state_hgrn, state_conv, w_in, attn_sink,
        lower_bound, hgrn_norm, conv_w, w_out, norm_mix, norm_ffn, w_gate_up, w_down, norm_final)
    return (y_prompt, y_sample, k_p, v_p, s_p, c_p, k_s, v_s, s_s, c_s)


_drawn_inputs = setup_inputs


def setup_inputs(seed=0):
    import zlib

    import numpy as np

    out = dict(_drawn_inputs(seed))
    spreads = {}
    factors = {'attn_sink': 2.998, 'hgrn_norm': 6.808, 'norm_ffn': 2.948, 'norm_final': 2.899}
    for name, (base, spread) in spreads.items():
        noise = np.random.default_rng([zlib.crc32(name.encode()), seed]).standard_normal(out[name].shape)
        drawn = base * np.exp(spread * noise) if base else spread * noise
        out[name] = __import__('jax').numpy.asarray(drawn.astype(out[name].dtype))
    for name, factor in factors.items():
        out[name] = (out[name] * factor).astype(out[name].dtype)
    return out
```

```python
from contextlib import ExitStack

import concourse.bass as bass
from concourse import mybir

ALU = mybir.AluOpType
ACT = mybir.ActivationFunctionType
AX = mybir.AxisListType
F32 = mybir.dt.float32
F32R = mybir.dt.float32r

P = 128
D_MODEL = 2048
SEQ = 256
DEPTH = 2
DEC_BATCH, DEC_SEQ = 8, 4
SAMP = DEC_BATCH * DEC_SEQ
TOK = SEQ + SAMP
WINDOW = 128
HEAD_DIM = 64
N_Q, N_KV = 16, 4
HG_HEADS, HG_D = 4, 128
CONV_K = 3
D_FF = 5632
PAST_LEN = 2048
ROT_DIM, ROPE_THETA = 16, 500000.0
NORM_EPS = 1e-6
LB_TINY = 1e-30
NEG_BIG = -1e30
ATTN_SCALE = HEAD_DIM ** -0.5
HG_SCALE = HG_D ** -0.5

KC = D_MODEL // P
IN_TILES = 40
SLAB_K, SLAB_N = 4, 256
FF_TILES = D_FF // P
FF_PART = (24, 20)
RING = 4
LEAD = 2

HQ, HF, HI, HG, Q0, Q1, KV, CB, CC, CH = (4 * i for i in range(10))

IN_SLABS, IN_GROUPS = IN_TILES // 2 * (KC // SLAB_K), IN_TILES // 2
OUT_SLABS, OUT_GROUPS = KC // 2 * 2, KC // 2
UP_SLABS = [f // 2 * 2 * (KC // SLAB_K) for f in FF_PART]
UP_GROUPS = [f for f in FF_PART]
DOWN_SLABS = [KC // 2 * (f // SLAB_K) for f in FF_PART]
DOWN_GROUPS = KC // 2
SLABS = IN_SLABS + 2 * OUT_SLABS + sum(UP_SLABS) + sum(DOWN_SLABS)
GROUPS = IN_GROUPS + 2 * OUT_GROUPS + sum(UP_GROUPS) + 2 * DOWN_GROUPS
FF_PAIRS = FF_TILES // 2

SUB, NSUB = 16, 8
DRING = 4
UNITS = 4

C_COS, C_SIN, C_ROT, C_ID, C_MASKP, C_HM, C_MC, C_MN, C_SM, C_VM, C_LB = range(11)
C_WIDTH = (TOK, TOK, P, P, 3 * P, P, P, SAMP, SAMP, DEC_BATCH, DEPTH * DEPTH)
C_AT = [sum(C_WIDTH[:i]) for i in range(len(C_WIDTH) + 1)]
P_GAIN, P_LB, P_HN, P_CW, P_SP, P_SS = range(6)
P_WIDTH = ((2 * DEPTH + 1) * KC, DEPTH * HG_HEADS, DEPTH * HG_HEADS, DEPTH * CONV_K * 4, DEPTH * N_Q, DEPTH * N_KV)
P_AT = [sum(P_WIDTH[:i]) for i in range(len(P_WIDTH) + 1)]


class Steps:

    def __init__(self, sem, names):
        self.sem, self.names, self.n = sem, names, 0
        self.start = len(names) + 1

    def step(self, name):
        assert self.names[self.n % len(self.names)] == name, (name, self.names[self.n % len(self.names)])
        self.n += 1
        return 1

    def at(self, trip, name):
        return trip * len(self.names) + (self.names.index(name) + 1 + self.start)

    def last(self, trip, name):
        return trip * len(self.names) + (self.names.index(name) + 2)

    def before(self, trip):
        return trip * len(self.names) + self.start


def build(nc, wstream, x_in, consts, params, conv_buf, kt_cache, v_cache, caches, s_cache,
          y_out, kp_out, vp_out, ks_out, vs_out, caches_out, hp_out, hs_out, cv_out):
    ctx = ExitStack()
    with ctx:
        def sem(name):
            return ctx.enter_context(nc.semaphore(name))

        place = [nc.sbuf_base + (-nc.sbuf_base) % 32]

        def size(shape):
            n = 4
            for d in shape[1:]:
                n *= d
            return n + (-n) % 32

        def sb(name, shape, dt=F32):
            t = nc.alloc_sbuf_tensor_at(name, shape, dt, offset=place[0])
            place[0] += size(shape)
            assert place[0] <= nc.sbuf_usable_end, (name, place[0], nc.sbuf_usable_end)
            return t

        def area(nbytes):
            at = place[0]
            place[0] += nbytes
            assert place[0] <= nc.sbuf_usable_end, (place[0], nc.sbuf_usable_end)
            return [at, at + nbytes]

        def sub(where, name, shape, dt=F32):
            t = nc.alloc_sbuf_tensor_at(name, shape, dt, offset=where[0])
            where[0] += size(shape)
            assert where[0] <= where[1], name
            return t

        cst = sb("cst", [P, C_AT[-1]])
        par = sb("par", [P, P_AT[-1]])
        mean_x = sb("mean_x", [P, P])
        mean_h = sb("mean_h", [P, P])
        eps = sb("eps", [P, 1])
        zero8 = sb("zero8", [P, NSUB])
        one_col = sb("one_col", [P, 2])
        oml = sb("oml", [P, DEPTH * HG_HEADS])
        lbc = sb("lbc", [P, DEPTH * HG_HEADS])
        lbt = sb("lbt", [P, 4, DEPTH * HG_HEADS])
        x = sb("x", [P, KC, TOK])
        xh = sb("xh", [P, KC, TOK], F32R)
        xl = sb("xl", [P, KC, TOK], F32R)
        mh = sb("mh", [P, 8, TOK], F32R)
        ml = sb("ml", [P, 8, TOK], F32R)
        rstd = sb("rstd", [P, TOK])
        raw = [sb(f"raw{i}", [P, SLAB_K, SLAB_N]) for i in range(RING)]
        whi = [sb(f"whi{i}", [P, SLAB_K, SLAB_N], F32R) for i in range(RING)]
        wlo = [sb(f"wlo{i}", [P, SLAB_K, SLAB_N], F32R) for i in range(RING)]

        wide = area(2 * max(FF_PART) * TOK * 4)
        ffn = list(wide)
        fh = sub(ffn, "fh", [P, max(FF_PART), TOK], F32R)
        fl = sub(ffn, "fl", [P, max(FF_PART), TOK], F32R)
        mix = list(wide)
        pj = sub(mix, "pj", [P, IN_TILES, TOK])
        tail = list(mix)
        over = [wide[0], wide[0] + size([P, Q0, TOK])]
        ah = sub(over, "ah", [P, 8, TOK], F32R)
        al = sub(over, "al", [P, 8, TOK], F32R)
        over = [wide[0] + size([P, Q0, TOK]), wide[0] + size([P, CB, TOK])]
        UPW = 2 + SEQ + 6 * DEC_BATCH
        up = sub(over, "up", [P, 4, UPW])
        yc = sub(over, "yc", [P, 4, UPW - 2])
        cnew = sub(over, "cnew", [P, 4, 18])
        cbuf = sub(over, "cbuf", [P, 4, 2 * DEC_BATCH])

        temp = area(23 * 1024)
        t = list(temp)
        gb = sub(t, "gb", [P, 2, TOK])
        gs = sub(t, "gs", [P, 2, TOK])
        gw = sub(t, "gw", [P, 2, TOK])
        fa = sub(t, "fa", [P, 2, TOK])
        sq2 = sub(t, "sq2", [P, 2, TOK])
        acc2 = sub(t, "acc2", [P, 2, TOK])
        rootx = sub(t, "rootx", [P, TOK])
        t, u = list(temp), list(tail)
        sig_f = sub(u, "sig_f", [P, TOK])
        sig_nf = sub(u, "sig_nf", [P, TOK])
        sig_q = sub(u, "sig_q", [P, TOK])
        sig_g = sub(u, "sig_g", [P, TOK])
        gate = sub(u, "gate", [P, TOK])
        f = sub(u, "f", [P, TOK])
        q = sub(u, "q", [P, TOK])
        f0 = sub(u, "f0", [P, TOK])
        g0 = sub(t, "g0", [P, TOK])
        pre = sub(t, "pre", [P, TOK])
        qp = sub(t, "qp", [P, TOK])
        D = [sub(t, f"D{i}", [P, TOK]) for i in range(DRING)]
        qpp = sub(t, "qpp", [P, P])
        AT = sub(t, "AT", [P, 2, P])
        ATs = sub(t, "ATs", [SAMP, SAMP])
        vst = sub(t, "vst", [P, TOK])
        vk = sub(t, "vk", [P, 4, P])
        vks = sub(t, "vks", [SAMP, 2, P])
        ct = sub(t, "ct", [P, NSUB])
        s1 = sub(t, "s1", [P, P])
        s2 = sub(t, "s2", [P, P])
        s0 = sub(t, "s0", [P, DEC_BATCH, P])
        vm = sub(t, "vm", [SAMP, 4, P])
        osb = sub(t, "osb", [P, TOK])
        t, u = list(temp), list(tail)
        qg = sub(u, "qg", [P, 4, TOK])
        krg = sub(u, "krg", [P, TOK])
        rs_a = sub(u, "rope_sin", [P, 2, TOK])
        sc = [sub(t, f"sc{i}", [P, 2, 3 * P]) for i in range(2)]
        pT = [sub(t, f"pT{i}", [P, 2, 3 * P]) for i in range(2)]
        kct = sub([temp[0], t[0]], "kct", [P, DEC_BATCH, WINDOW])
        vct = sub([temp[0] + 2 * size(sc[0].shape), t[0]], "vct", [P, DEC_BATCH, P])
        kvt = sub(t, "kvt", [P, 2, P])
        vnt = sub(t, "vnt", [SAMP, P])
        qs = sub(t, "qs", [P, DEC_BATCH, 4, DEC_SEQ])
        sst = sub(t, "sst", [P, 2, P])
        ss = sub(t, "ss", [P, 2, WINDOW + SAMP])
        pts = sub(t, "pts", [P, 2, P])
        ptn = sub(t, "ptn", [SAMP, 2, P])
        asb = sub(t, "asb", [P, 4, SAMP])
        st = [sub(t, f"st{i}", [P, 6, 4]) for i in range(2)]
        sts = sub(t, "sts", [P, 6, 2])
        vst_a = sub(t, "vst_a", [P, TOK])
        rt_a = sub(t, "rope_cos", [P, 2, TOK])

        gp = [ctx.enter_context(nc.psum_tensor(f"gp{i}", [P, 512], F32)) for i in range(4)]
        mb = [ctx.enter_context(nc.psum_tensor(f"mb{i}", [P, 512], F32)) for i in range(4)]

        def const(i):
            return cst[:, C_AT[i]:C_AT[i + 1]]

        cos, sin, rot, ident = const(C_COS), const(C_SIN), const(C_ROT), const(C_ID)

        def pcol(i, k):
            return par[:, bass.ds(P_AT[i] + k, 1)]

        par_loaded = sem("parameters_loaded")
        x_loaded = [sem(f"x_loaded{i}") for i in range(4)]
        const_loaded = sem("constants_loaded")
        ones_set = sem("ones_set")
        lb_steps = sem("lower_bound_steps")
        lb_exp = sem("lower_bound_exponentials")
        raw_ready = [sem(f"raw_ready{i}") for i in range(RING)]
        hi_ready = sem("hi_ready")
        lo_ready = sem("lo_ready")
        slab_used = sem("slab_used")
        group_out = sem("group_out")
        xh_new = sem("xh_new")
        xl_new = sem("xl_new")
        sq_new = sem("square_steps")
        ms_ready = sem("mean_square_ready")
        root_ready = sem("root_ready")
        rstd_ready = sem("rstd_ready")
        sig_ready = sem("gate_sigmoid_ready")
        gw_steps = sem("gate_product_steps")
        fh_ready = sem("ffn_hi_ready")
        fl_ready = sem("ffn_lo_ready")
        y_ready = sem("y_ready")
        y_stored = sem("y_stored")

        hv = Steps(sem("hgrn_vector"), ["zero", "k", "q", "f", "k3", "D1", "D2", "D3", "pre", "qp", "ct"]
                   + [f"D{r}" for r in range(4, SUB)] + [f"K{i}" for i in range(2, NSUB + 1)]
                   + ["qpp0", "qpp", "atd", "at", "ats", "ssa", "s2", "ri", "o1", "o2", "ssb", "ml"])
        hs = Steps(sem("hgrn_sigmoids"), ["sig_f", "sig_nf", "sig_q", "sig_g"])
        ha = Steps(sem("hgrn_scalar"), ["vt", "kt", "s1", "osq", "osb", "root", "mh"])
        hp = Steps(sem("hgrn_gpsimd"), ["vst", "g0a", "g0b", "f0", "f0a", "f0b", "gate", "vma", "vmb"])
        ht = Steps(sem("hgrn_tensor"), ["vt"] + [f"A{r}" for r in range(SUB)] + [f"O{i}" for i in range(1, NSUB)]
                   + ["kt", "s1", "ssa", "out", "ssb", "norm"])
        g0_zero = sem("hgrn_starts_cleared")
        h_load = sem("hgrn_state_loaded")
        h_store = sem("hgrn_state_stored")
        cvv = Steps(sem("conv_vector"), ["pad", "u", "us", "w0", "w1", "w2", "cm", "cms", "ml"])
        cva = Steps(sem("conv_scalar"), ["buf", "hi"])
        cvp = Steps(sem("conv_gpsimd"), ["new", "stored"])
        c_load = sem("conv_buffer_loaded")
        c_store = sem("conv_buffer_stored")
        av = Steps(sem("attn_vector"), [s for n in range(5) for s in (f"sin{n}", f"rot{n}")]
                   + ["sc0", "mx0", "mm0", "nm0", "ds0", "den0", "rec0", "p0"]
                   + ["sc1", "mx1", "mm1", "nm1", "ds1", "den1", "rec1", "p1", "al0"]
                   + ["sc2", "mx2", "mm2", "nm2", "ds2", "den2", "rec2", "p2", "al1"]
                   + ["sc3", "mx3", "mm3", "nm3", "ds3", "den3", "rec3", "p3", "al2", "al3"]
                   + ["ssn", "smx", "smm", "snm", "sds", "sden", "srec", "sp", "asb", "sal"])
        aa = Steps(sem("attn_scalar"), ["es0", "kvt", "pT0", "es1", "ah0", "pT1", "es2", "ah1", "pT2", "es3", "ah2",
                                        "pT3", "ah3", "sst", "ses", "pts", "sah"])
        ap_ = Steps(sem("attn_gpsimd"), [f"cos{n}" for n in range(5)] + ["vst", "qs", "stored"])
        at = Steps(sem("attn_tensor"), [f"R{n}" for n in range(5)]
                   + ["sc0", "tv", "sc1", "pt0", "pv0", "sc2", "pt1", "pv1", "sc3", "pt2", "pv2", "pt3", "pv3"]
                   + ["st", "ss", "pts", "pvs"])
        a_load = [sem("kt_cache_loaded"), sem("v_cache_loaded")]
        a_store = sem("attn_stored")
        cache_moved = sem("cache_moved")
        waits_passed = sem("waits_passed")
        def hgrn_in(l):
            return l * GROUPS + (Q0 // 2 + 2)

        def conv_in(l):
            return l * GROUPS + (IN_TILES // 2 + 2)

        def attn_in(l):
            return l * GROUPS + (CB // 2 + 2)

        mix_hi, mix_lo = (mh, ah), (ml, al)

        def hgrn_over(eng, l):
            for s in (hv, ha, hs, hp, ht):
                eng.wait_ge(s.sem, s.before(l * HG_HEADS + HG_HEADS))
            apart(eng)

        def hgrn_stored(eng, l):
            eng.wait_ge(h_store, l * (32 * HG_HEADS) + (32 * HG_HEADS + 32))
            apart(eng)

        block = ctx.enter_context(nc.Block())

        def apart(eng):
            eng.sem_inc(waits_passed, 1)

        @block.sync
        def _(sp):
            def load(n, slot, src):
                sp.wait_ge(lo_ready, n + 1)
                sp.dma_start(raw[slot][:], wstream[bass.ds(src, 1)].rearrange("s p (c n) -> p (s c) n", c=SLAB_K)
                             ).then_inc(raw_ready[slot], 16)

            with sp.Fori(0, DEPTH * SLABS // RING) as i:
                for s in range(RING):
                    load(i * RING + s, s, i * RING + s)
            for s in range(LEAD):
                load(DEPTH * SLABS + s, s, s)
            for c in range(4):
                sp.wait_ge(y_ready, c + 1)
                sp.dma_start(y_out[:, 4 * c:4 * c + 4, :], x[:, 4 * c:4 * c + 4, :]).then_inc(y_stored, 16)
            sp.wait_ge(y_stored, 64)

        @block.scalar
        def _(a):
            a.dma_start(par[:], params).then_inc(par_loaded, 16)
            for c in range(4):
                a.dma_start(x[:, 4 * c:4 * c + 4, :], x_in[:, 4 * c:4 * c + 4, :]).then_inc(x_loaded[c], 16)
            for s in (hs, ha, cva, aa):
                a.sem_inc(s.sem, s.start)
            a.sem_inc(h_store, 32)

            def hi(n4, s):
                slot = s % RING
                a.wait_ge(raw_ready[slot], (n4 + s // RING) * 16 + 16)
                a.wait_ge(slab_used, n4 * RING + (s + 1))
                a.activation(whi[slot][:], raw[slot][:], ACT.Copy).then_inc(hi_ready, 1)

            def scale_hi(tn, j, g):
                a.wait_ge(group_out, g)
                apart(a)
                for c in range(2):
                    m = a.activation(xh[:, bass.ds(2 * j + c, 1), :], x[:, bass.ds(2 * j + c, 1), :], ACT.Copy,
                                     scale=pcol(P_GAIN, tn * KC + 2 * j + c))
                m.then_inc(xh_new, 1)

            def root(tn):
                a.wait_ge(ms_ready, tn + 1)
                a.activation(rootx[:], mb[3][:, 0:TOK], ACT.Sqrt, bias=eps[:]).then_inc(root_ready, 1)

            def sigmoids(T, h, used):
                for name, dst, src, sgn in (("sig_f", sig_f, HF, 1.0), ("sig_nf", sig_nf, HF, -1.0),
                                            ("sig_q", sig_q, HQ, 1.0), ("sig_g", sig_g, HG, 1.0)):
                    used(name)
                    apart(a)
                    a.activation(dst[:], pj[:, bass.ds(src + h, 1), :].rearrange("p o t -> p (o t)"), ACT.Sigmoid,
                                 scale=sgn).then_inc(hs.sem, hs.step(name))

            def hgrn(T, h, l, last):
                yield
                a.wait_ge(ht.sem, ht.last(T, "norm"))
                a.wait_ge(ht.sem, ht.at(T, "vt"))
                a.activation(vk[:, 0:2, :], mb[2][:, 0:256].rearrange("p (m e) -> p m e", m=2), ACT.Copy)
                a.activation(vks[:, 0, :], mb[1][0:SAMP, 64:192], ACT.Copy).then_inc(ha.sem, ha.step("vt"))
                for _ in range(2):
                    yield
                if not last:
                    def used(name):
                        if name == "sig_g":
                            a.wait_ge(hp.sem, hp.at(T, "gate"))
                        else:
                            a.wait_ge(hv.sem, hv.at(T, {"sig_f": "f", "sig_nf": "k", "sig_q": "q"}[name]))
                    sigmoids(T + 1, h + 1, used)
                for _ in range(8):
                    yield
                a.wait_ge(ht.sem, ht.at(T, "kt"))
                a.activation(vk[:, 2:4, :], mb[2][:, 256:512].rearrange("p (m e) -> p m e", m=2), ACT.Copy)
                a.activation(vks[:, 1, :], mb[1][0:SAMP, 192:320], ACT.Copy).then_inc(ha.sem, ha.step("kt"))
                yield
                a.wait_ge(ht.sem, ht.at(T, "s1"))
                a.activation(s1[:], mb[2][:, 0:P], ACT.Copy).then_inc(ha.sem, ha.step("s1"))
                yield
                a.wait_ge(ht.sem, ht.at(T, "out"))
                a.activation(f0[:], mb[3][:, 0:TOK], ACT.Square).then_inc(ha.sem, ha.step("osq"))
                a.activation(osb[:], mb[3][:, 0:TOK], ACT.Copy).then_inc(ha.sem, ha.step("osb"))
                a.activation(one_col[:, 0:1], eps[:], ACT.Sqrt)
                yield
                a.wait_ge(ht.sem, ht.at(T, "norm"))
                a.activation(f0[:], mb[0][:, 0:TOK], ACT.Sqrt, bias=eps[:]).then_inc(ha.sem, ha.step("root"))
                a.wait_ge(hv.sem, hv.at(T, "o2"))
                apart(a)
                a.activation(mh[:, bass.ds(h, 1), :].rearrange("p o t -> p (o t)"), osb[:], ACT.Copy
                             ).then_inc(ha.sem, ha.step("mh"))
                a.wait_ge(hv.sem, hv.at(T, "ssb"))
                a.dma_start(hp_out[bass.ds(T, 1)].rearrange("o d e -> d (o e)"), s2[:]).then_inc(h_store, 16)
                a.dma_start(hs_out[bass.ds(T, 1)].rearrange("o d b e -> d (o b) e"), s0[:]).then_inc(h_store, 16)
                yield

            def conv(T):
                for _ in range(6):
                    yield
                a.wait_ge(c_load, T * 16 + 16)
                a.wait_ge(cvv.sem, cvv.at(T, "pad"))
                for c in range(4):
                    m = a.activation(up[:, c, 2 + SEQ:].rearrange("p (b j) -> p b j", j=6)[:, :, 0:2],
                                     cbuf[:, c, :].rearrange("p (b j) -> p b j", j=2), ACT.Copy)
                m.then_inc(cva.sem, cva.step("buf"))
                for _ in range(5):
                    yield
                a.wait_ge(cvv.sem, cvv.at(T, "cms"))
                a.activation(ah[:, 0:4, :], pj[:, CB:CB + 4, :], ACT.Copy).then_inc(cva.sem, cva.step("hi"))
                yield

            def attn(T, gg, l):
                out = mix_hi[gg]
                if gg == 0:
                    hgrn_over(a, l)
                a.wait_ge(av.sem, av.before(T))

                def exps(u):
                    a.wait_ge(av.sem, av.at(T, f"ds{u}"))
                    s_, w = st[u % 2], sc[u % 2]
                    for i in range(2):
                        a.activation(w[:, i, 0:P], w[:, i, 0:P], ACT.Exp, bias=s_[:, 1, i:i + 1],
                                     accum_out=s_[:, 3, i:i + 1])
                        a.activation(w[:, i, P:3 * P], w[:, i, P:3 * P], ACT.Exp, bias=s_[:, 1, 2 + i:3 + i],
                                     accum_out=s_[:, 3, 2 + i:3 + i])
                    a.activation(s_[:, 4, :], s_[:, 2, :], ACT.Exp).then_inc(aa.sem, aa.step(f"es{u}"))

                def turned(u):
                    a.wait_ge(at.sem, at.at(T, f"pt{u}"))
                    for i in range(2):
                        m = a.activation(pT[u % 2][:, i, :], mb[2 + i][:, 0:3 * P], ACT.Copy)
                    m.then_inc(aa.sem, aa.step(f"pT{u}"))

                def out_hi(u):
                    a.wait_ge(at.sem, at.at(T, f"pv{u}"))
                    a.activation(out[:, 4 + u, 0:SEQ], mb[2][:, 0:SEQ], ACT.Copy).then_inc(aa.sem, aa.step(f"ah{u}"))

                for _ in range(3):
                    yield
                exps(0)
                a.wait_ge(at.sem, at.at(T, "tv"))
                a.activation(kvt[:], mb[2][:, 0:2 * P].rearrange("p (m e) -> p m e", m=2), ACT.Copy)
                a.activation(vnt[:], mb[3][0:SAMP, 0:P], ACT.Copy).then_inc(aa.sem, aa.step("kvt"))
                yield
                for u in range(3):
                    turned(u)
                    yield
                    exps(u + 1)
                    out_hi(u)
                    yield
                turned(3)
                yield
                out_hi(3)
                if gg == 0:
                    hgrn_stored(a, l)
                a.wait_ge(at.sem, at.at(T, "st"))
                a.activation(sst[:, 0, :], mb[0][:, 0:P], ACT.Copy)
                a.activation(sst[:, 1, :], mb[1][:, 0:P], ACT.Copy).then_inc(aa.sem, aa.step("sst"))
                yield
                yield
                a.wait_ge(av.sem, av.at(T, "sds"))
                a.activation(ss[:, 0, :], ss[:, 0, :], ACT.Exp, bias=sts[:, 1, 0:1], accum_out=sts[:, 3, 0:1])
                a.activation(ss[:, 1, :], ss[:, 1, :], ACT.Exp, bias=sts[:, 1, 1:2], accum_out=sts[:, 3, 1:2])
                a.activation(sts[:, 4, :], sts[:, 2, :], ACT.Exp).then_inc(aa.sem, aa.step("ses"))
                yield
                a.wait_ge(at.sem, at.at(T, "pts"))
                a.activation(pts[:], mb[2][:, 0:256].rearrange("p (g r) -> p g r", g=2), ACT.Copy)
                a.activation(ptn[:], mb[2][0:SAMP, 256:512].rearrange("p (g r) -> p g r", g=2), ACT.Copy
                             ).then_inc(aa.sem, aa.step("pts"))
                yield
                a.wait_ge(av.sem, av.at(T, "asb"))
                a.activation(out[:, 4:8, SEQ:TOK], asb[:], ACT.Copy).then_inc(aa.sem, aa.step("sah"))
                yield

            def group(n4, s0, m, fills=()):
                for s in range(m):
                    hi(n4, s0 + s + LEAD)
                    for fill in fills:
                        next(fill, None)

            def ffn_part(l, n4, g, part):
                def pair(i, norm=False):
                    m4 = n4 + i * 2
                    group(m4, 0, 4)
                    if norm:
                        root(l * 2 + 1)
                    a.wait_ge(group_out, g + i * 2 + 3)
                    a.activation(gs[:], gb[:], ACT.Sigmoid).then_inc(sig_ready, 1)
                    group(m4, 4, 4)
                    a.wait_ge(group_out, g + i * 2 + 4)
                    apart(a)
                    a.activation(fh[:, bass.ds(2 * i, 2), :], fa[:], ACT.Copy).then_inc(fh_ready, 1)

                if part == 0:
                    pair(0, norm=True)
                with a.Fori(1 - part, FF_PART[part] // 2) as i:
                    pair(i)

            a.wait_ge(ones_set, 4)
            a.wait_ge(par_loaded, 16)
            hi(0, 0)
            for j in range(KC // 2):
                a.wait_ge(x_loaded[j // 2], 16)
                for c in range(2 * j, 2 * j + 2):
                    m = a.activation(xh[:, c, :], x[:, c, :], ACT.Copy, scale=par[:, P_AT[P_GAIN] + c:P_AT[P_GAIN] + c + 1])
                m.then_inc(xh_new, 1)
                if j == 3:
                    hi(0, 1)
            a.wait_ge(lb_steps, 2 * DEPTH)
            a.activation(lbt[:, 2, :], lbt[:, 1, :], ACT.Exp).then_inc(lb_exp, 1)
            with a.Fori(0, DEPTH) as l:
                n4 = l * (SLABS // RING)
                g = l * GROUPS
                group(n4, 0, 4)
                root(l * 2)
                group(n4, 4, 4)
                with a.Fori(1, 4) as i:
                    group(n4 + i * 2, 0, 8)
                a.wait_ge(group_out, hgrn_in(l))
                sigmoids(l * HG_HEADS, 0, lambda name: None)

                def head(h, last):
                    fill = hgrn(l * HG_HEADS + h, h, l, last)
                    group(n4 + h * 2 + 8, 0, 8, (fill, fill))
                    for _ in fill:
                        pass

                with a.Fori(0, HG_HEADS - 1) as h:
                    head(h, False)
                head(HG_HEADS - 1, True)
                fill = attn(l * 2, 0, l)
                group(n4 + 16, 0, 16, (fill,))
                for _ in fill:
                    pass
                n4 += IN_SLABS // RING
                g += IN_GROUPS
                fill = attn(l * 2 + 1, 1, l)
                group(n4, 0, 16, (fill, conv(l)))
                for _ in fill:
                    pass
                n4 += OUT_SLABS // RING
                g += OUT_GROUPS
                with a.Fori(0, 4) as i:
                    for b in range(2):
                        group(n4 + i, 2 * b, 2)
                        scale_hi(l * 2 + 1, 2 * i + b, g + i * 2 + (b + 3))
                n4 += OUT_SLABS // RING
                g += OUT_GROUPS
                for part in range(2):
                    ffn_part(l, n4, g, part)
                    n4 += UP_SLABS[part] // RING
                    g += UP_GROUPS[part]
                    k = FF_PART[part] // SLAB_K
                    gpb = 2 if k % 2 == 0 else 4
                    with a.Fori(0, DOWN_GROUPS // gpb) as i:
                        for b in range(gpb):
                            group(n4 + i * (k * gpb // RING), b * k, k)
                            if part == 1:
                                scale_hi(l * 2 + 2, gpb * i + b, g + i * gpb + (b + 3))
                    n4 += DOWN_SLABS[part] // RING
                    g += DOWN_GROUPS
            root(2 * DEPTH)

        @block.vector
        def _(v):
            v.sem_inc(lo_ready, RING)
            v.sem_inc(group_out, 2)
            for s in (hv, cvv, av):
                v.sem_inc(s.sem, s.start)

            def lo(n4, s):
                slot = s % RING
                v.wait_ge(hi_ready, n4 * RING + (s + 1))
                v.tensor_tensor(wlo[slot][:], raw[slot][:], whi[slot][:].bitcast(F32), ALU.subtract
                                ).then_inc(lo_ready, 1)

            def group(n4, s0, m, fills=()):
                for s in range(m):
                    lo(n4, s0 + s + LEAD)
                    for fill in fills:
                        next(fill, None)

            def used(n4, s):
                v.wait_ge(slab_used, n4 * RING + (s + RING))

            def scale_lo(tn, j):
                v.wait_ge(xh_new, tn * (KC // 2) + j + 1)
                for c in range(2):
                    xc = bass.ds(2 * j + c, 1)
                    m = v.scalar_tensor_tensor(xl[:, xc, :], x[:, xc, :], pcol(P_GAIN, tn * KC + 2 * j + c),
                                               xh[:, xc, :].bitcast(F32), ALU.mult, ALU.subtract)
                m.then_inc(xl_new, 1)

            def finish_rstd(tn):
                v.wait_ge(root_ready, tn + 1)
                v.reciprocal(rstd[:], rootx[:]).then_inc(rstd_ready, 1)
                v.wait_ge(rstd_ready, tn + 1)
                apart(v)

            def out_proj(bank, tile):
                for c in range(2):
                    m = v.tensor_tensor(pj[:, bass.ds(tile + c, 1), :].rearrange("p o t -> p (o t)"),
                                        gp[2 * bank + c][:, 0:TOK], rstd[:], ALU.mult)
                m.then_inc(group_out, 1)

            def out_add(bank, j):
                for c in range(2):
                    xc = x[:, bass.ds(2 * j + c, 1), :].rearrange("p o t -> p (o t)")
                    m = v.tensor_tensor(xc, gp[2 * bank + c][:, 0:TOK], xc, ALU.add)
                m.then_inc(group_out, 1)

            def blocks(t_, n=SEQ // SUB, r=SUB):
                return t_[:, 0:n * r].rearrange("p (n r) -> p n r", r=r)

            def sblocks(t_):
                return t_[:, SEQ:TOK].rearrange("p (n r) -> p n r", r=DEC_SEQ)

            def hgrn(T, h, l):
                v.wait_ge(group_out, hgrn_in(l))
                v.wait_ge(ha.sem, ha.before(T))
                v.wait_ge(hp.sem, hp.before(T))
                v.wait_ge(ht.sem, ht.before(T))
                v.memset(mb[0][:, 256:512], 0.0).then_inc(hv.sem, hv.step("zero"))
                v.wait_ge(hs.sem, hs.at(T, "sig_nf"))
                v.tensor_scalar(D[0][:], sig_nf[:], oml[:, bass.ds(T, 1)], None, ALU.mult
                                ).then_inc(hv.sem, hv.step("k"))
                v.wait_ge(hs.sem, hs.at(T, "sig_q"))
                v.scalar_tensor_tensor(q[:], pj[:, bass.ds(HQ + h, 1), :].rearrange("p o t -> p (o t)"), HG_SCALE,
                                       sig_q[:], ALU.mult, ALU.mult).then_inc(hv.sem, hv.step("q"))
                v.wait_ge(hs.sem, hs.at(T, "sig_f"))
                v.tensor_scalar(f[:], sig_f[:], oml[:, bass.ds(T, 1)], lbc[:, bass.ds(T, 1)], ALU.mult, ALU.add
                                ).then_inc(hv.sem, hv.step("f"))
                v.wait_ge(hv.sem, hv.at(T, "k"))
                for i in range(1, DRING):
                    m = v.tensor_copy(D[i][:], D[0][:])
                m.then_inc(hv.sem, hv.step("k3"))

                def decay(r):
                    v.wait_ge(hv.sem, hv.at(T, f"D{r - 1}" if r > 1 else "k3"))
                    if r >= DRING:
                        v.wait_ge(ht.sem, ht.at(T, f"A{r - DRING}"))
                    new, old = D[r % DRING], D[(r - 1) % DRING]
                    if r < DEC_SEQ:
                        v.tensor_tensor(sblocks(new)[:, :, 0:r], sblocks(old)[:, :, 0:r],
                                        sblocks(f)[:, :, r:r + 1].to_broadcast([P, DEC_BATCH, r]), ALU.mult)
                    v.tensor_tensor(blocks(new)[:, :, 0:r], blocks(old)[:, :, 0:r],
                                    blocks(f)[:, :, r:r + 1].to_broadcast([P, SEQ // SUB, r]), ALU.mult
                                    ).then_inc(hv.sem, hv.step(f"D{r}"))

                decay(1)
                yield
                yield
                decay(2)
                decay(3)
                yield
                v.wait_ge(hp.sem, hp.at(T, "f0b"))
                v.tensor_tensor_scan(pre[:], f0[:], g0[:], 0.0, ALU.mult, ALU.add).then_inc(hv.sem, hv.step("pre"))
                v.wait_ge(hv.sem, hv.at(T, "pre"))
                v.tensor_tensor(qp[:], q[:], pre[:], ALU.mult).then_inc(hv.sem, hv.step("qp"))
                tot = blocks(pre)[:, :, SUB - 1]
                v.tensor_tensor_scan(ct[:], tot[:, NSUB:2 * NSUB], zero8[:], 1.0, ALU.mult, ALU.add
                                     ).then_inc(hv.sem, hv.step("ct"))
                for r in range(4, SUB, 2):
                    yield
                    decay(r)
                    decay(r + 1)

                def older(i):
                    last = D[(SUB - 1) % DRING]
                    v.wait_ge(hv.sem, hv.at(T, f"K{i - 1}" if i > 2 else "D15"))
                    v.wait_ge(ht.sem, ht.at(T, f"O{i - 3}" if i > 4 else "A14"))
                    n = SUB * (i - 1)

                    def tiles(b):
                        return b[:, 0:SEQ].rearrange("p (m s) -> p m s", m=2)
                    new, old = tiles(D[i % 3]), tiles(D[(i - 1) % 3] if i > 2 else last)
                    v.tensor_copy(new[:, :, n:n + SUB], tiles(last)[:, :, n:n + SUB])
                    v.tensor_tensor(new[:, :, 0:n], old[:, :, 0:n],
                                    tiles(pre)[:, :, n + SUB - 1:n + SUB].to_broadcast([P, 2, n]), ALU.mult
                                    ).then_inc(hv.sem, hv.step(f"K{i}"))

                yield
                older(2)
                older(3)
                older(4)
                older(5)
                yield
                older(6)
                older(7)
                older(8)
                v.wait_ge(hv.sem, hv.at(T, "ct"))
                v.tensor_copy(qpp[:, 0:SUB], qp[:, P:P + SUB]).then_inc(hv.sem, hv.step("qpp0"))
                v.tensor_tensor(blocks(qpp, NSUB)[:, 1:, :], blocks(qp)[:, NSUB + 1:, :],
                                ct[:, 0:NSUB - 1].unsqueeze(2).to_broadcast([P, NSUB - 1, SUB]), ALU.mult
                                ).then_inc(hv.sem, hv.step("qpp"))
                yield
                v.wait_ge(ht.sem, ht.at(T, f"O{NSUB - 1}"))
                for m_ in range(2):
                    m = v.tensor_tensor(
                        AT[:, m_, :].rearrange("p (i r) -> p i r", r=SUB),
                        mb[0][:, m_ * P:(m_ + 1) * P].rearrange("p (r i) -> p i r", r=SUB),
                        const(C_HM).rearrange("p (i r) -> p i r", r=SUB), ALU.mult)
                m.then_inc(hv.sem, hv.step("atd"))
                v.wait_ge(hv.sem, hv.at(T, "atd"))
                v.tensor_tensor(AT[:].rearrange("p m t -> p (m t)"), mb[0][:, 256:512],
                                AT[:].rearrange("p m t -> p (m t)"), ALU.add).then_inc(hv.sem, hv.step("at"))
                v.tensor_tensor(ATs[:].rearrange("p (b r) -> p b r", r=DEC_SEQ),
                                mb[3][0:SAMP, 320:320 + SAMP].rearrange("p (r b) -> p b r", r=DEC_SEQ),
                                const(C_SM)[0:SAMP, :].rearrange("p (b r) -> p b r", r=DEC_SEQ), ALU.mult
                                ).then_inc(hv.sem, hv.step("ats"))
                yield

                def sample_state(half, name, bank):
                    v.wait_ge(ht.sem, ht.at(T, name))
                    v.wait_ge(ht.sem, ht.at(T, "out"))
                    for b in range(4 * half, 4 * half + 4):
                        m = v.scalar_tensor_tensor(s0[:, b, :], s0[:, b, :], sblocks(pre)[:, b, DEC_SEQ - 1:DEC_SEQ],
                                                   mb[bank][:, (b % 4) * P:(b % 4 + 1) * P], ALU.mult, ALU.add)
                    m.then_inc(hv.sem, hv.step(name))

                yield
                sample_state(0, "ssa", 1)
                v.wait_ge(ha.sem, ha.at(T, "s1"))
                v.wait_ge(h_store, T * 32 + 32)
                v.scalar_tensor_tensor(s2[:], s1[:], ct[:, NSUB - 1:NSUB], mb[2][:, P:2 * P], ALU.mult, ALU.add
                                       ).then_inc(hv.sem, hv.step("s2"))
                yield
                v.wait_ge(ha.sem, ha.at(T, "root"))
                v.reciprocal(qp[:], f0[:]).then_inc(hv.sem, hv.step("ri"))
                v.wait_ge(hv.sem, hv.at(T, "ri"))
                v.scalar_tensor_tensor(osb[:], osb[:], pcol(P_HN, T), qp[:], ALU.mult, ALU.mult
                                       ).then_inc(hv.sem, hv.step("o1"))
                v.wait_ge(hv.sem, hv.at(T, "o1"))
                v.wait_ge(hp.sem, hp.at(T, "gate"))
                v.tensor_tensor(osb[:], osb[:], gate[:], ALU.mult).then_inc(hv.sem, hv.step("o2"))
                sample_state(1, "ssb", 2)
                v.wait_ge(ha.sem, ha.at(T, "mh"))
                v.tensor_tensor(ml[:, bass.ds(h, 1), :].rearrange("p o t -> p (o t)"), osb[:],
                                mh[:, bass.ds(h, 1), :].rearrange("p o t -> p (o t)").bitcast(F32), ALU.subtract
                                ).then_inc(hv.sem, hv.step("ml"))
                yield

            def conv(T):
                sview = up[:, :, 2 + SEQ:].rearrange("p c (b j) -> p c b j", j=6)
                for _ in range(5):
                    yield
                v.wait_ge(at.sem, at.at(T * 2 + 1, "R4"))
                v.wait_ge(ap_.sem, ap_.at(T * 2 + 1, "vst"))
                v.memset(up[:, :, 0:2], 0.0).then_inc(cvv.sem, cvv.step("pad"))
                v.tensor_tensor(up[:, :, 2:2 + SEQ], pj[:, CC:CC + 4, 0:SEQ], pj[:, CH:CH + 4, 0:SEQ], ALU.mult
                                ).then_inc(cvv.sem, cvv.step("u"))
                yield
                for c in range(4):
                    m = v.tensor_tensor(sview[:, c, :, 2:6],
                                        pj[:, CC + c, SEQ:TOK].rearrange("p (b t) -> p b t", t=DEC_SEQ),
                                        pj[:, CH + c, SEQ:TOK].rearrange("p (b t) -> p b t", t=DEC_SEQ), ALU.mult)
                m.then_inc(cvv.sem, cvv.step("us"))
                yield
                v.wait_ge(cvv.sem, cvv.at(T, "us"))
                v.wait_ge(cva.sem, cva.at(T, "buf"))
                for c in range(4):
                    m = v.tensor_scalar(yc[:, c, :], up[:, c, 0:UPW - 2], pcol(P_CW, T * 12 + c), None, ALU.mult)
                m.then_inc(cvv.sem, cvv.step("w0"))
                yield
                for j in (1, 2):
                    v.wait_ge(cvv.sem, cvv.at(T, f"w{j - 1}"))
                    for c in range(4):
                        m = v.scalar_tensor_tensor(yc[:, c, :], up[:, c, j:UPW - 2 + j], pcol(P_CW, T * 12 + (4 * j + c)),
                                                   yc[:, c, :], ALU.mult, ALU.add)
                    m.then_inc(cvv.sem, cvv.step(f"w{j}"))
                    yield
                v.wait_ge(cvv.sem, cvv.at(T, "w2"))
                v.tensor_tensor(pj[:, CB:CB + 4, 0:SEQ], pj[:, CB:CB + 4, 0:SEQ], yc[:, :, 0:SEQ], ALU.mult
                                ).then_inc(cvv.sem, cvv.step("cm"))
                for c in range(4):
                    gated = pj[:, CB + c, SEQ:TOK].rearrange("p (b t) -> p b t", t=DEC_SEQ)
                    m = v.tensor_tensor(gated, gated,
                                        yc[:, c, SEQ:SEQ + 6 * DEC_BATCH].rearrange("p (b j) -> p b j", j=6)[:, :, 2:6],
                                        ALU.mult)
                m.then_inc(cvv.sem, cvv.step("cms"))
                yield
                yield
                v.wait_ge(cva.sem, cva.at(T, "hi"))
                v.tensor_tensor(al[:, 0:4, :], pj[:, CB:CB + 4, :], ah[:, 0:4, :].bitcast(F32), ALU.subtract
                                ).then_inc(cvv.sem, cvv.step("ml"))
                yield

            def attn(T, gg, l):
                def rope(n):
                    v.wait_ge(at.sem, at.at(T, f"R{n}"))
                    v.tensor_tensor(rs_a[:, n % 2, :], mb[n % 4][:, 0:TOK], sin, ALU.mult
                                    ).then_inc(av.sem, av.step(f"sin{n}"))
                    v.wait_ge(av.sem, av.at(T, f"sin{n}"))
                    v.wait_ge(ap_.sem, ap_.at(T, f"cos{n}"))
                    if n == 4:
                        v.tensor_tensor(krg[:], rs_a[:, 0, :], rt_a[:, 0, :], ALU.add).then_inc(av.sem, av.step("rot4"))
                        return
                    dst = n // 2 * 64
                    for half in range(2):
                        src = slice(64 * half, 64 * half + 64)
                        m = v.tensor_tensor(qg[dst:dst + 64, 2 * (n % 2) + half, :], rs_a[src, n % 2, :],
                                            rt_a[src, n % 2, :], ALU.add)
                    m.then_inc(av.sem, av.step(f"rot{n}"))

                out, out_l = mix_hi[gg], mix_lo[gg]
                if gg == 0:
                    hgrn_over(v, l)
                v.wait_ge(at.sem, at.before(T))
                v.wait_ge(ap_.sem, ap_.before(T))
                for n in range(4):
                    rope(n)
                yield
                rope(4)

                def scores(u):
                    s_, w = st[u % 2], sc[u % 2]
                    v.wait_ge(at.sem, at.at(T, f"sc{u}"))
                    for i in range(2):
                        m = v.scalar_tensor_tensor(w[:, i, :], mb[i][:, 0:3 * P], ATTN_SCALE, const(C_MASKP),
                                                   ALU.mult, ALU.add)
                    m.then_inc(av.sem, av.step(f"sc{u}"))
                    v.wait_ge(av.sem, av.at(T, f"sc{u}"))
                    v.tensor_reduce(s_[:, 0, 0:2], w[:, :, 0:P], AX.X, ALU.max)
                    v.tensor_reduce(s_[:, 0, 2:4], w[:, :, P:3 * P], AX.X, ALU.max).then_inc(av.sem, av.step(f"mx{u}"))
                    sink = par[:, bass.ds(P_AT[P_SP] + T * 8 + 2 * u, 2)].unsqueeze(1).to_broadcast([P, 2, 2])

                    def both(k):
                        return s_[:, k, :].rearrange("p (b i) -> p b i", b=2)
                    v.wait_ge(av.sem, av.at(T, f"mx{u}"))
                    v.tensor_tensor(both(5), both(0), sink, ALU.max).then_inc(av.sem, av.step(f"mm{u}"))
                    v.wait_ge(av.sem, av.at(T, f"mm{u}"))
                    v.tensor_scalar(s_[:, 1, :], s_[:, 5, :], -1.0, None, ALU.mult).then_inc(av.sem, av.step(f"nm{u}"))
                    v.wait_ge(av.sem, av.at(T, f"nm{u}"))
                    v.tensor_tensor(both(2), both(1), sink, ALU.add).then_inc(av.sem, av.step(f"ds{u}"))

                def probs(u):
                    s_, w = st[u % 2], sc[u % 2]
                    v.wait_ge(aa.sem, aa.at(T, f"es{u}"))
                    v.tensor_tensor(s_[:, 0, :], s_[:, 3, :], s_[:, 4, :], ALU.add).then_inc(av.sem, av.step(f"den{u}"))
                    v.wait_ge(av.sem, av.at(T, f"den{u}"))
                    v.reciprocal(s_[:, 5, :], s_[:, 0, :]).then_inc(av.sem, av.step(f"rec{u}"))
                    v.wait_ge(av.sem, av.at(T, f"rec{u}"))
                    v.tensor_tensor(w[:, :, 0:P], w[:, :, 0:P],
                                    s_[:, 5, 0:2].unsqueeze(2).to_broadcast([P, 2, P]), ALU.mult)
                    v.tensor_tensor(w[:, :, P:3 * P], w[:, :, P:3 * P],
                                    s_[:, 5, 2:4].unsqueeze(2).to_broadcast([P, 2, 2 * P]), ALU.mult
                                    ).then_inc(av.sem, av.step(f"p{u}"))

                def out_lo(u):
                    v.wait_ge(aa.sem, aa.at(T, f"ah{u}"))
                    v.tensor_tensor(out_l[:, 4 + u, 0:SEQ], mb[2][:, 0:SEQ], out[:, 4 + u, 0:SEQ].bitcast(F32),
                                    ALU.subtract).then_inc(av.sem, av.step(f"al{u}"))

                yield
                scores(0)
                yield
                probs(0)
                yield
                scores(1)
                yield
                probs(1)
                out_lo(0)
                yield
                scores(2)
                yield
                probs(2)
                out_lo(1)
                yield
                scores(3)
                yield
                probs(3)
                out_lo(2)
                yield
                yield
                out_lo(3)
                yield
                if gg == 0:
                    hgrn_stored(v, l)
                v.wait_ge(at.sem, at.at(T, "ss"))
                for g in range(2):
                    v.scalar_tensor_tensor(ss[:, g, 0:WINDOW], mb[0][:, 256 + g * P:256 + (g + 1) * P], ATTN_SCALE,
                                           const(C_MC), ALU.mult, ALU.add)
                    m = v.scalar_tensor_tensor(ss[:, g, WINDOW:], mb[g][:, P:P + SAMP],
                                               ATTN_SCALE, const(C_MN), ALU.mult, ALU.add)
                m.then_inc(av.sem, av.step("ssn"))
                v.wait_ge(av.sem, av.at(T, "ssn"))
                v.tensor_reduce(sts[:, 0, :], ss[:], AX.X, ALU.max).then_inc(av.sem, av.step("smx"))
                v.wait_ge(av.sem, av.at(T, "smx"))
                sink = par[:, bass.ds(P_AT[P_SS] + T * 2, 2)]
                v.tensor_tensor(sts[:, 5, :], sts[:, 0, :], sink, ALU.max).then_inc(av.sem, av.step("smm"))
                v.wait_ge(av.sem, av.at(T, "smm"))
                v.tensor_scalar(sts[:, 1, :], sts[:, 5, :], -1.0, None, ALU.mult).then_inc(av.sem, av.step("snm"))
                v.wait_ge(av.sem, av.at(T, "snm"))
                v.tensor_tensor(sts[:, 2, :], sts[:, 1, :], sink, ALU.add).then_inc(av.sem, av.step("sds"))
                yield
                v.wait_ge(aa.sem, aa.at(T, "ses"))
                v.tensor_tensor(sts[:, 0, :], sts[:, 3, :], sts[:, 4, :], ALU.add).then_inc(av.sem, av.step("sden"))
                v.wait_ge(av.sem, av.at(T, "sden"))
                v.reciprocal(sts[:, 5, :], sts[:, 0, :]).then_inc(av.sem, av.step("srec"))
                v.wait_ge(av.sem, av.at(T, "srec"))
                v.tensor_tensor(ss[:], ss[:], sts[:, 5, :].unsqueeze(2).to_broadcast([P, 2, WINDOW + SAMP]), ALU.mult
                                ).then_inc(av.sem, av.step("sp"))
                yield
                yield
                v.wait_ge(at.sem, at.at(T, "pvs"))
                for g in range(2):
                    for half in range(2):
                        rows = mb[1][0:64, g * P:(g + 1) * P].rearrange("p (b i t) -> p i b t", b=DEC_BATCH, i=4)
                        for c in range(2):
                            m = v.tensor_copy(asb[64 * half:64 * half + 64, 2 * g + c, :]
                                              .rearrange("p (b t) -> p b t", t=DEC_SEQ), rows[:, 2 * c + half, :, :])
                m.then_inc(av.sem, av.step("asb"))
                v.wait_ge(aa.sem, aa.at(T, "sah"))
                v.tensor_tensor(out_l[:, 4:8, SEQ:TOK], asb[:], out[:, 4:8, SEQ:TOK].bitcast(F32), ALU.subtract
                                ).then_inc(av.sem, av.step("sal"))
                yield

            def ffn_part(l, n4, part, pair0):
                def one(i, norm=False):
                    m4 = n4 + i * 2
                    pair = l * FF_PAIRS + i + pair0
                    group(m4, 0, 4)
                    if norm:
                        finish_rstd(l * 2 + 1)
                    used(m4, 4)
                    for c in range(2):
                        m = v.tensor_tensor(gb[:, c, :], gp[c][:, 0:TOK], rstd[:], ALU.mult)
                    m.then_inc(group_out, 1)
                    group(m4, 4, 4)
                    used(m4, 8)
                    v.wait_ge(gw_steps, pair * 2 + 2)
                    for c in range(2):
                        m = v.tensor_tensor(fa[:, c, :], gp[2 + c][:, 0:TOK], gw[:, c, :], ALU.mult)
                    m.then_inc(group_out, 1)
                    v.wait_ge(fh_ready, pair + 1)
                    v.tensor_tensor(fl[:, bass.ds(2 * i, 2), :], fa[:], fh[:, bass.ds(2 * i, 2), :].bitcast(F32),
                                    ALU.subtract).then_inc(fl_ready, 1)

                if part == 0:
                    one(0, norm=True)
                with v.Fori(1 - part, FF_PART[part] // 2) as i:
                    one(i)

            v.wait_ge(par_loaded, 16)
            nh = HG_HEADS
            step = [0]

            def lb_step(ins):
                step[0] += 1
                ins.then_inc(lb_steps, 1)
                v.wait_ge(lb_steps, step[0])

            def lb_col(l):
                return par[:, P_AT[P_LB] + l * nh:P_AT[P_LB] + (l + 1) * nh]

            top = lbt[:, 0, 0:nh]
            lb_step(v.tensor_copy(top, lb_col(0)))
            for l in range(1, DEPTH):
                lb_step(v.tensor_tensor(top, top, lb_col(l), ALU.max))
            for l in range(DEPTH):
                lb_step(v.tensor_tensor(lbt[:, 1, l * nh:(l + 1) * nh], lb_col(l), top, ALU.subtract))
            for j in range(KC // 2):
                v.wait_ge(x_loaded[j // 2], 16)
                v.wait_ge(xh_new, j + 1)
                for c in range(2 * j, 2 * j + 2):
                    m = v.scalar_tensor_tensor(xl[:, c, :], x[:, c, :], par[:, P_AT[P_GAIN] + c:P_AT[P_GAIN] + c + 1],
                                               xh[:, c, :].bitcast(F32), ALU.mult, ALU.subtract)
                m.then_inc(xl_new, 1)
                if j == 1:
                    lo(0, 0)
                if j == 3:
                    lo(0, 1)
            v.wait_ge(lb_exp, 1)
            lb_step(v.tensor_copy(lbt[:, 0, 0:nh], lbt[:, 2, 0:nh]))
            for l in range(1, DEPTH):
                lb_step(v.tensor_tensor(lbt[:, 0, 0:nh], lbt[:, 0, 0:nh], lbt[:, 2, l * nh:(l + 1) * nh], ALU.add))
            lb_step(v.reciprocal(lbt[:, 3, 0:nh], lbt[:, 0, 0:nh]))
            for l in range(DEPTH):
                cur = lbt[:, 1, l * nh:(l + 1) * nh]
                lb_step(v.memset(cur, 0.0))
                for j in range(1, l + 1):
                    lb_step(v.tensor_tensor(cur, cur, lbt[:, 2, j * nh:(j + 1) * nh], ALU.add))
                lb_step(v.tensor_tensor(cur, cur, lbt[:, 3, 0:nh], ALU.mult))
                lb_step(v.tensor_scalar(oml[:, l * nh:(l + 1) * nh], cur, -1.0, 1.0, ALU.mult, ALU.add))
                lb_step(v.tensor_scalar(lbc[:, l * nh:(l + 1) * nh], cur, LB_TINY, None, ALU.max))

            with v.Fori(0, DEPTH) as l:
                n4 = l * (SLABS // RING)
                g = l * GROUPS
                def in_groups(i, norm=False):
                    for b in range(2):
                        group(n4 + i * 2, 4 * b, 4)
                        if norm and b == 0:
                            finish_rstd(l * 2)
                        used(n4 + i * 2, 4 * b + 4)
                        out_proj(b, 4 * i + 2 * b)

                in_groups(0, norm=True)
                with v.Fori(1, 4) as i:
                    in_groups(i)
                v.wait_ge(const_loaded, 16)
                with v.Fori(0, HG_HEADS) as h:
                    fill = hgrn(l * HG_HEADS + h, h, l)
                    next(fill)
                    for b in range(2):
                        group(n4 + h * 2 + 8, 4 * b, 3, (fill, fill))
                        group(n4 + h * 2 + 8, 4 * b + 3, 1, (fill,))
                        used(n4 + h * 2 + 8, 4 * b + 4)
                        out_proj(b, 4 * h + 2 * b + 16)
                        next(fill, None)
                    for _ in fill:
                        pass
                fill = attn(l * 2, 0, l)
                for i in range(2):
                    for b in range(2):
                        group(n4 + 16 + 2 * i, 4 * b, 4, (fill,))
                        used(n4 + 16 + 2 * i, 4 * b + 4)
                        out_proj(b, 32 + 4 * i + 2 * b)
                for _ in fill:
                    pass
                n4 += IN_SLABS // RING
                g += IN_GROUPS
                fill, fill_conv = attn(l * 2 + 1, 1, l), conv(l)
                for b in range(OUT_GROUPS):
                    group(n4, 2 * b, 2, (fill, fill_conv))
                    used(n4, 2 * b + 2)
                    out_add(b % 2, b)
                for _ in fill:
                    pass
                n4 += OUT_SLABS // RING
                g += OUT_GROUPS
                with v.Fori(0, 4) as i:
                    for b in range(2):
                        group(n4 + i, 2 * b, 2)
                        used(n4 + i, 2 * b + 2)
                        out_add(b, 2 * i + b)
                        scale_lo(l * 2 + 1, 2 * i + b)
                n4 += OUT_SLABS // RING
                g += OUT_GROUPS
                pair0 = 0
                for part in range(2):
                    ffn_part(l, n4, part, pair0)
                    pair0 += FF_PART[part] // 2
                    n4 += UP_SLABS[part] // RING
                    k = FF_PART[part] // SLAB_K
                    gpb = 2 if k % 2 == 0 else 4
                    with v.Fori(0, DOWN_GROUPS // gpb) as i:
                        for b in range(gpb):
                            group(n4 + i * (k * gpb // RING), b * k, k)
                            used(n4 + i * (k * gpb // RING), b * k + k)
                            out_add(b % 2, gpb * i + b)
                            if part == 1:
                                scale_lo(l * 2 + 2, gpb * i + b)
                    n4 += DOWN_SLABS[part] // RING
            finish_rstd(2 * DEPTH)
            for c in range(KC):
                col = P_AT[P_GAIN] + 2 * DEPTH * KC + c
                m = v.scalar_tensor_tensor(x[:, c, :], x[:, c, :], par[:, col:col + 1], rstd[:], ALU.mult, ALU.mult)
                if c % 4 == 3:
                    m.then_inc(y_ready, 1)

        @block.gpsimd
        def _(e):
            e.memset(mean_x[:], 1.0 / D_MODEL).then_inc(ones_set, 1)
            e.memset(mean_h[:], 1.0 / HG_D).then_inc(ones_set, 1)
            e.memset(eps[:], NORM_EPS).then_inc(ones_set, 1)
            e.memset(zero8[:], 0.0).then_inc(ones_set, 1)
            for s in (hp, cvp, ap_):
                e.sem_inc(s.sem, s.start)
            PER = 1 + KC

            def squares_start(tn):
                e.memset(acc2[:], 0.0).then_inc(sq_new, 1)

            def squares(tn, j):
                xs = x[:, bass.ds(2 * j, 2), :]
                apart(e)
                e.tensor_tensor(sq2[:], xs, xs, ALU.mult).then_inc(sq_new, 1)
                e.wait_ge(sq_new, tn * PER + 2 * j + 2)
                e.tensor_tensor(acc2[:], acc2[:], sq2[:], ALU.add).then_inc(sq_new, 1)
                e.wait_ge(sq_new, tn * PER + 2 * j + 3)

            def hgrn(T, h, l):
                e.wait_ge(group_out, hgrn_in(l))
                e.wait_ge(ht.sem, ht.last(T, "vt"))
                apart(e)
                e.tensor_copy(vst[:], pj[:, bass.ds(HI + h, 1), :].rearrange("p o t -> p (o t)")
                              ).then_inc(hp.sem, hp.step("vst"))
                e.wait_ge(hv.sem, hv.at(T, "f"))
                apart(e)
                e.tensor_copy(g0[:, 0:SEQ:SUB], f[:, 0:SEQ:SUB]).then_inc(hp.sem, hp.step("g0a"))
                e.tensor_copy(g0[:, SEQ:TOK:DEC_SEQ], f[:, SEQ:TOK:DEC_SEQ]).then_inc(hp.sem, hp.step("g0b"))
                e.tensor_copy(f0[:], f[:]).then_inc(hp.sem, hp.step("f0"))
                e.wait_ge(hp.sem, hp.at(T, "f0"))
                apart(e)
                e.memset(f0[:, 0:SEQ:SUB], 0.0).then_inc(hp.sem, hp.step("f0a"))
                e.memset(f0[:, SEQ:TOK:DEC_SEQ], 0.0).then_inc(hp.sem, hp.step("f0b"))
                e.wait_ge(h_store, T * 32 + 32)
                apart(e)
                e.dma_start(s0[:], s_cache[bass.ds(T, 1)].rearrange("o d b e -> d (o b) e")).then_inc(h_load, 16)
                e.wait_ge(hs.sem, hs.at(T, "sig_g"))
                apart(e)
                e.tensor_tensor(gate[:], pj[:, bass.ds(HG + h, 1), :].rearrange("p o t -> p (o t)"), sig_g[:], ALU.mult
                                ).then_inc(hp.sem, hp.step("gate"))
                e.wait_ge(ha.sem, ha.at(T, "vt"))
                apart(e)

                def masked(half, name):
                    e.tensor_tensor(vm[:], vks[:, 0:1, :].to_broadcast([SAMP, 4, P]),
                                    const(C_VM)[0:SAMP, 4 * half:4 * half + 4].unsqueeze(2).to_broadcast([SAMP, 4, P]),
                                    ALU.mult).then_inc(hp.sem, hp.step(name))
                masked(0, "vma")
                e.wait_ge(ht.sem, ht.at(T, "ssa"))
                apart(e)
                masked(1, "vmb")

            def conv(T):
                e.wait_ge(at.sem, at.at(T * 2 + 1, "R4"))
                e.wait_ge(ap_.sem, ap_.at(T * 2 + 1, "vst"))
                apart(e)
                e.dma_start(cbuf[:], conv_buf[bass.ds(T, 1)].rearrange("o p c j -> p (o c) j")).then_inc(c_load, 16)
                e.wait_ge(cvv.sem, cvv.at(T, "us"))
                apart(e)
                e.tensor_copy(cnew[:, :, 0:2], up[:, :, SEQ:SEQ + 2])
                for c in range(4):
                    m = e.tensor_copy(cnew[:, c, 2:18].rearrange("p (b j) -> p b j", j=2),
                                      up[:, c, 2 + SEQ:].rearrange("p (b j) -> p b j", j=6)[:, :, 4:6])
                m.then_inc(cvp.sem, cvp.step("new"))
                e.wait_ge(cvp.sem, cvp.at(T, "new"))
                e.dma_start(cv_out[bass.ds(T, 1)].rearrange("o p c j -> p (o c) j"), cnew[:]).then_inc(c_store, 16)
                e.wait_ge(c_store, T * 16 + 16)
                e.sem_inc(cvp.sem, cvp.step("stored"))

            def attn(T, gg, l):
                if gg == 0:
                    hgrn_over(e, l)
                e.wait_ge(group_out, attn_in(l))
                e.wait_ge(at.sem, at.before(T))
                e.wait_ge(av.sem, av.before(T))
                e.wait_ge(aa.sem, aa.before(T))
                apart(e)
                for n in range(5):
                    if n >= 2:
                        e.wait_ge(av.sem, av.at(T, f"rot{n - 2}"))
                    tile = 4 * gg + Q0 + n if n < 4 else gg + KV
                    apart(e)
                    e.tensor_tensor(rt_a[:, n % 2, :], pj[:, bass.ds(tile, 1), :].rearrange("p o t -> p (o t)"), cos,
                                    ALU.mult).then_inc(ap_.sem, ap_.step(f"cos{n}"))
                e.tensor_copy(vst_a[:], pj[:, bass.ds(gg + (KV + 2), 1), :].rearrange("p o t -> p (o t)")
                              ).then_inc(ap_.sem, ap_.step("vst"))
                e.wait_ge(av.sem, av.at(T, "rot4"))
                apart(e)
                for i in range(4):
                    m = e.tensor_copy(qs[:, :, i, :], qg[:, i, SEQ:TOK].rearrange("p (b t) -> p b t", t=DEC_SEQ))
                m.then_inc(ap_.sem, ap_.step("qs"))
                for src, prompt, sample in ((krg, kp_out, ks_out), (vst_a, vp_out, vs_out)):
                    e.wait_ge(ap_.sem, ap_.at(T, "vst"))
                    apart(e)
                    e.dma_start(prompt[bass.ds(T, 1)].rearrange("o p t -> p (o t)"), src[:, SEQ - WINDOW:SEQ]
                                ).then_inc(a_store, 16)
                    e.dma_start(sample[bass.ds(T, 1)].rearrange("o p t -> p (o t)"), src[:, SEQ:TOK]).then_inc(a_store, 16)
                if gg == 1:
                    conv(l)
                e.wait_ge(at.sem, at.at(T, "pt3"))
                apart(e)
                e.dma_start(kct[:], kt_cache[bass.ds(T, 1)].rearrange("o p b s -> p (o b) s")).then_inc(a_load[0], 16)
                e.wait_ge(at.sem, at.at(T, "pv3"))
                apart(e)
                e.dma_start(vct[:], v_cache[bass.ds(T, 1)].rearrange("o s b d -> s (o b) d")).then_inc(a_load[1], 16)
                e.wait_ge(a_store, T * 64 + 64)
                e.wait_ge(ap_.sem, ap_.at(T, "qs"))
                e.sem_inc(ap_.sem, ap_.step("stored"))

            e.dma_start(cst[:], consts).then_inc(const_loaded, 16)
            squares_start(0)
            e.wait_ge(sq_new, 1)
            for j in range(KC // 2):
                e.wait_ge(x_loaded[j // 2], 16)
                squares(0, j)
            e.dma_start(caches_out, caches[:, DEC_SEQ:, :]).then_inc(cache_moved, 16)
            with e.Fori(0, DEPTH) as l:
                e.wait_ge(root_ready, l * 2 + 1)
                apart(e)
                e.memset(g0[:], 0.0).then_inc(g0_zero, 1)
                e.wait_ge(g0_zero, l + 1)
                apart(e)
                e.wait_ge(const_loaded, 16)
                with e.Fori(0, HG_HEADS) as h:
                    hgrn(l * HG_HEADS + h, h, l)
                for gg in range(2):
                    attn(l * 2 + gg, gg, l)
                g = l * GROUPS + (IN_GROUPS + OUT_GROUPS)
                e.wait_ge(aa.sem, aa.before(l * 2 + 2))
                e.wait_ge(av.sem, av.before(l * 2 + 2))
                e.wait_ge(at.sem, at.before(l * 2 + 2))
                apart(e)
                squares_start(l * 2 + 1)
                e.wait_ge(sq_new, (l * 2 + 1) * PER + 1)
                apart(e)
                with e.Fori(0, KC // 2) as j:
                    e.wait_ge(group_out, g + j + 3)
                    squares(l * 2 + 1, j)
                g += OUT_GROUPS
                pair0 = 0
                for part in range(2):
                    with e.Fori(0, FF_PART[part] // 2) as i:
                        pair = l * FF_PAIRS + i + pair0
                        e.wait_ge(sig_ready, pair + 1)
                        e.tensor_tensor(gw[:], gb[:], gs[:], ALU.mult).then_inc(gw_steps, 1)
                        e.wait_ge(gw_steps, pair * 2 + 1)
                        e.tensor_tensor(gw[:], gw[:], rstd[:].unsqueeze(1).to_broadcast([P, 2, TOK]), ALU.mult
                                        ).then_inc(gw_steps, 1)
                    pair0 += FF_PART[part] // 2
                    g += UP_GROUPS[part] + DOWN_GROUPS
                g -= DOWN_GROUPS
                e.wait_ge(root_ready, l * 2 + 2)
                apart(e)
                squares_start(l * 2 + 2)
                e.wait_ge(sq_new, (l * 2 + 2) * PER + 1)
                apart(e)
                with e.Fori(0, KC // 2) as j:
                    e.wait_ge(group_out, g + j + 3)
                    squares(l * 2 + 2, j)
            e.wait_ge(cache_moved, 16)

        @block.tensor
        def _(t):
            t.sem_inc(slab_used, RING)
            for s in (ht, at):
                t.sem_inc(s.sem, s.start)

            def group(n4, s0, m, g, bank, mov, fill=None, halves=True):
                t.wait_ge(group_out, g + 1)
                for s in range(m):
                    slot = (s0 + s) % RING
                    mov(s)
                    t.wait_ge(lo_ready, n4 * RING + (s0 + s + 1 + RING))
                    for c in range(2):
                        out = gp[2 * bank + c][:, 0:TOK]
                        for k in range(SLAB_K):
                            w_hi = whi[slot][:, k, c * P:(c + 1) * P]
                            w_lo = wlo[slot][:, k, c * P:(c + 1) * P]
                            mv_hi, mv_lo = mov(s, k)
                            first, last = s == 0 and k == 0, s == m - 1 and k == SLAB_K - 1
                            t.matmul(out, w_hi, mv_hi, start=first, stop=False)
                            t.matmul(out, w_hi, mv_lo, start=False, stop=False)
                            mm = t.matmul(out, w_lo, mv_hi, start=False, stop=last)
                        if c == 1:
                            mm.then_inc(slab_used, 1)
                        if fill is not None and (halves or c == 1):
                            next(fill, None)

            def from_x(tn):
                def mov(s, k=None):
                    if k is None:
                        t.wait_ge(xl_new, tn * (KC // 2) + 2 * (s + 1))
                        return
                    return xh[:, SLAB_K * s + k, :], xl[:, SLAB_K * s + k, :]
                return mov

            def from_mix(hi_, lo_, done):
                def mov(s, k=None):
                    if k is None:
                        done(s)
                        return
                    return hi_[:, SLAB_K * s + k, :], lo_[:, SLAB_K * s + k, :]
                return mov

            def from_ffn(base):
                def mov(s, k=None):
                    if k is None:
                        t.wait_ge(fl_ready, base + 2 * (s + 1))
                        return
                    return fh[:, SLAB_K * s + k, :], fl[:, SLAB_K * s + k, :]
                return mov

            def mean_square(tn):
                t.wait_ge(sq_new, (tn + 1) * (1 + KC))
                t.matmul(mb[3][:, 0:TOK], mean_x[:], acc2[:, 0, :], start=True, stop=False)
                t.matmul(mb[3][:, 0:TOK], mean_x[:], acc2[:, 1, :], start=False, stop=True).then_inc(ms_ready, 1)

            def hgrn(T, h, l):
                yield
                t.wait_ge(hp.sem, hp.at(T, "vst"))
                t.wait_ge(hv.sem, hv.last(T, "ssb"))
                for m_ in range(2):
                    t.transpose(mb[2][:, m_ * P:(m_ + 1) * P], vst[:, m_ * P:(m_ + 1) * P], ident)
                t.transpose(mb[1][0:SAMP, 64:192], vst[:, SEQ:TOK], ident).then_inc(ht.sem, ht.step("vt"))

                def within(r):
                    t.wait_ge(hv.sem, hv.at(T, f"D{r}" if r else "q"))
                    d = D[r % DRING]
                    if r < DEC_SEQ:
                        t.matmul(mb[3][0:SAMP, 320 + r * DEC_BATCH:320 + (r + 1) * DEC_BATCH], d[:, SEQ:TOK],
                                 q[:, SEQ + r:TOK:DEC_SEQ], start=True, stop=True)
                    for m_ in range(2):
                        mm = t.matmul(mb[0][:, m_ * P + r * NSUB:m_ * P + (r + 1) * NSUB], d[:, m_ * P:(m_ + 1) * P],
                                      q[:, m_ * P + r:(m_ + 1) * P:SUB], start=True, stop=True)
                    mm.then_inc(ht.sem, ht.step(f"A{r}"))

                for r in range(0, SUB, 2):
                    yield
                    within(r)
                    within(r + 1)

                def before(i):
                    t.wait_ge(hv.sem, hv.at(T, f"K{i}" if i > 1 else "qp"))
                    n = SUB * i
                    d = D[i % 3] if i > 1 else D[(SUB - 1) % DRING]
                    for m_ in range(2):
                        lo_ = m_ * P
                        mm = t.matmul(mb[0][0:n, 256 + lo_ + n:256 + lo_ + n + SUB], d[:, lo_:lo_ + n],
                                      qp[:, lo_ + n:lo_ + n + SUB], start=True, stop=True)
                    mm.then_inc(ht.sem, ht.step(f"O{i}"))

                yield
                for i in range(1, 5):
                    before(i)
                yield
                for i in range(5, 8):
                    before(i)
                t.wait_ge(hv.sem, hv.at(T, f"K{NSUB}"))
                t.wait_ge(ha.sem, ha.at(T, "vt"))
                for m_ in range(2):
                    t.transpose(mb[2][:, 256 + m_ * P:256 + (m_ + 1) * P], D[NSUB % 3][:, m_ * P:(m_ + 1) * P], ident)
                t.transpose(mb[1][0:SAMP, 192:320], D[DEC_SEQ - 1][:, SEQ:TOK], ident).then_inc(ht.sem, ht.step("kt"))
                yield
                t.wait_ge(ha.sem, ha.at(T, "kt"))
                t.matmul(mb[2][:, 0:P], vk[:, 2, :], vk[:, 0, :], start=True, stop=True)
                t.matmul(mb[2][:, P:2 * P], vk[:, 3, :], vk[:, 1, :], start=True, stop=True
                         ).then_inc(ht.sem, ht.step("s1"))
                t.wait_ge(hp.sem, hp.at(T, "vma"))
                t.matmul(mb[1][:], vks[:, 1, :], vm[:].rearrange("p b e -> p (b e)"), start=True, stop=True
                         ).then_inc(ht.sem, ht.step("ssa"))
                yield
                t.wait_ge(hv.sem, hv.at(T, "ats"))
                t.wait_ge(ha.sem, ha.at(T, "s1"))
                t.wait_ge(h_load, T * 16 + 16)
                t.matmul(mb[3][:, 0:P], vk[:, 0, :], AT[:, 0, :], start=True, stop=True)
                t.matmul(mb[3][:, P:2 * P], vk[:, 1, :], AT[:, 1, :], start=True, stop=False)
                t.matmul(mb[3][:, P:2 * P], s1[:], qpp[:], start=False, stop=True)
                t.matmul(mb[3][:, SEQ:TOK], vks[:, 0, :], ATs[:], start=True, stop=False)
                for b in range(DEC_BATCH):
                    cols = slice(SEQ + DEC_SEQ * b, SEQ + DEC_SEQ * (b + 1))
                    mm = t.matmul(mb[3][:, cols], s0[:, b, :], qp[:, cols], start=False, stop=(b == DEC_BATCH - 1))
                mm.then_inc(ht.sem, ht.step("out"))
                yield
                t.wait_ge(hp.sem, hp.at(T, "vmb"))
                t.wait_ge(hv.sem, hv.at(T, "s2"))
                t.matmul(mb[2][:], vks[:, 1, :], vm[:].rearrange("p b e -> p (b e)"), start=True, stop=True
                         ).then_inc(ht.sem, ht.step("ssb"))
                t.wait_ge(ha.sem, ha.at(T, "osq"))
                t.matmul(mb[0][:, 0:TOK], mean_h[:], f0[:], start=True, stop=True).then_inc(ht.sem, ht.step("norm"))
                yield

            def attn(T, gg, l):
                t.wait_ge(group_out, attn_in(l))
                if gg == 0:
                    t.wait_ge(hv.sem, hv.last(l * HG_HEADS + HG_HEADS, "ssb"))
                    t.wait_ge(ha.sem, ha.last(l * HG_HEADS + HG_HEADS, "root"))
                t.wait_ge(av.sem, av.before(T))
                t.wait_ge(aa.sem, aa.before(T))

                def partners(n):
                    tile = 4 * gg + Q0 + n if n < 4 else gg + KV
                    t.matmul(mb[n % 4][:, 0:TOK], rot, pj[:, bass.ds(tile, 1), :].rearrange("p o t -> p (o t)"),
                             start=True, stop=True).then_inc(at.sem, at.step(f"R{n}"))

                def score(u):
                    rows = slice(64 * (u // 2), 64 * (u // 2) + 64)
                    t.wait_ge(av.sem, av.at(T, f"sc{u - 1}" if u else "rot4"))
                    for i in range(2):
                        h = 2 * (u % 2) + i
                        t.matmul(mb[i][:, 0:P], qg[rows, h, 0:P], krg[rows, 0:P], start=True, stop=True)
                        mm = t.matmul(mb[i][:, P:3 * P], qg[rows, h, P:2 * P], krg[rows, 0:2 * P], start=True, stop=True)
                    mm.then_inc(at.sem, at.step(f"sc{u}"))

                def turn(u):
                    if u:
                        t.wait_ge(av.sem, av.at(T, f"al{u - 1}"))
                    else:
                        t.wait_ge(aa.sem, aa.at(T, "kvt"))
                    t.wait_ge(av.sem, av.at(T, f"p{u}"))
                    for i in range(2):
                        for c in range(3):
                            mm = t.transpose(mb[2 + i][:, c * P:(c + 1) * P], sc[u % 2][:, i, c * P:(c + 1) * P], ident)
                    mm.then_inc(at.sem, at.step(f"pt{u}"))

                def values(u):
                    t.wait_ge(aa.sem, aa.at(T, f"pT{u}"))
                    cols = slice(64 * (u // 2), 64 * (u // 2) + 64)
                    for i in range(2):
                        o, w = mb[2][64 * i:64 * i + 64, 0:SEQ], pT[u % 2][:, i, :]
                        t.matmul(o[:, 0:P], kvt[:, 0, cols], w[:, 0:P], start=True, stop=True)
                        t.matmul(o[:, P:SEQ], kvt[:, 0, cols], w[:, P:2 * P], start=True, stop=False)
                        mm = t.matmul(o[:, P:SEQ], kvt[:, 1, cols], w[:, 2 * P:3 * P], start=False, stop=True)
                    mm.then_inc(at.sem, at.step(f"pv{u}"))

                for n in range(4):
                    partners(n)
                yield
                t.wait_ge(av.sem, av.at(T, "sin0"))
                partners(4)
                yield
                score(0)
                yield
                t.wait_ge(ap_.sem, ap_.at(T, "vst"))
                for m_ in range(2):
                    t.transpose(mb[2][:, m_ * P:(m_ + 1) * P], vst_a[:, m_ * P:(m_ + 1) * P], ident)
                t.transpose(mb[3][0:SAMP, 0:P], vst_a[:, SEQ:TOK], ident).then_inc(at.sem, at.step("tv"))
                yield
                for u in range(3):
                    score(u + 1)
                    turn(u)
                    yield
                    values(u)
                    yield
                turn(3)
                yield
                values(3)
                t.wait_ge(av.sem, av.at(T, "sc3"))
                t.wait_ge(a_load[0], T * 16 + 16)
                t.wait_ge(ap_.sem, ap_.at(T, "qs"))
                for g in range(2):
                    rows = slice(64 * g, 64 * g + 64)
                    for b in range(DEC_BATCH):
                        t.matmul(mb[g][:, 16 * b:16 * b + 16], kct[rows, b, :],
                                 qs[rows, b, :, :].rearrange("p i t -> p (i t)"), start=True, stop=True)
                    mm = t.matmul(mb[g][:, P:P + SAMP],
                                  qs[rows, :, :, :].rearrange("p b i t -> p (b i t)"), krg[rows, SEQ:TOK],
                                  start=True, stop=True)
                mm.then_inc(at.sem, at.step("st"))
                yield
                t.wait_ge(aa.sem, aa.at(T, "sst"))
                for g in range(2):
                    mm = t.transpose(mb[0][:, 256 + g * P:256 + (g + 1) * P], sst[:, g, :], ident)
                mm.then_inc(at.sem, at.step("ss"))
                yield
                yield
                t.wait_ge(av.sem, av.at(T, "sp"))
                for g in range(2):
                    t.transpose(mb[2][:, g * P:(g + 1) * P], ss[:, g, 0:WINDOW], ident)
                    mm = t.transpose(mb[2][0:SAMP, 256 + g * P:256 + (g + 1) * P], ss[:, g, WINDOW:], ident)
                mm.then_inc(at.sem, at.step("pts"))
                yield
                t.wait_ge(aa.sem, aa.at(T, "pts"))
                t.wait_ge(a_load[1], T * 16 + 16)
                for g in range(2):
                    rows = slice(64 * g, 64 * g + 64)
                    t.matmul(mb[1][0:64, g * P:(g + 1) * P], vnt[:, rows], ptn[:, g, :], start=True, stop=False)
                    for b in range(DEC_BATCH):
                        mm = t.matmul(mb[1][0:64, g * P + 16 * b:g * P + 16 * b + 16], vct[:, b, rows],
                                      pts[:, g, 16 * b:16 * b + 16], start=False, stop=(b == DEC_BATCH - 1))
                mm.then_inc(at.sem, at.step("pvs"))
                yield

            t.wait_ge(ones_set, 4)
            with t.Fori(0, DEPTH) as l:
                n4 = l * (SLABS // RING)
                g = l * GROUPS
                xin = from_x(l * 2)
                group(n4, 0, 4, g, 0, xin)
                mean_square(l * 2)
                group(n4, 4, 4, g + 1, 1, xin)
                with t.Fori(1, 4) as i:
                    for b in range(2):
                        group(n4 + i * 2, 4 * b, 4, g + i * 2 + b, b, xin)
                t.wait_ge(const_loaded, 16)
                with t.Fori(0, HG_HEADS) as h:
                    fill = hgrn(l * HG_HEADS + h, h, l)
                    for b in range(2):
                        group(n4 + h * 2 + 8, 4 * b, 4, g + h * 2 + (8 + b), b, xin, fill)
                    for _ in fill:
                        pass
                fill = attn(l * 2, 0, l)
                for i in range(2):
                    for b in range(2):
                        group(n4 + 16 + 2 * i, 4 * b, 4, g + (16 + 2 * i + b), b, xin, fill, halves=False)
                for _ in fill:
                    pass
                n4 += IN_SLABS // RING
                g += IN_GROUPS

                def half_a(s):
                    if s == 0:
                        t.wait_ge(hv.sem, hv.before(l * HG_HEADS + HG_HEADS))
                    else:
                        t.wait_ge(av.sem, av.before(l * 2 + 1))

                def half_b(s):
                    if s == 0:
                        t.wait_ge(cvv.sem, cvv.before(l + 1))
                    else:
                        t.wait_ge(av.sem, av.before(l * 2 + 2))

                fill = attn(l * 2 + 1, 1, l)
                for b in range(OUT_GROUPS):
                    group(n4, 2 * b, 2, g + b, b % 2, from_mix(mh, ml, half_a), fill, halves=False)
                for _ in fill:
                    pass
                n4 += OUT_SLABS // RING
                g += OUT_GROUPS
                with t.Fori(0, 4) as i:
                    for b in range(2):
                        group(n4 + i, 2 * b, 2, g + i * 2 + b, b, from_mix(ah, al, half_b))
                n4 += OUT_SLABS // RING
                g += OUT_GROUPS
                pair0 = 0
                for part in range(2):
                    if part == 0:
                        group(n4, 0, 4, g, 0, from_x(l * 2 + 1))
                        mean_square(l * 2 + 1)
                        group(n4, 4, 4, g + 1, 1, from_x(l * 2 + 1))
                    with t.Fori(1 - part, FF_PART[part] // 2) as i:
                        for b in range(2):
                            group(n4 + i * 2, 4 * b, 4, g + i * 2 + b, b, from_x(l * 2 + 1))
                    n4 += UP_SLABS[part] // RING
                    g += UP_GROUPS[part]
                    k = FF_PART[part] // SLAB_K
                    gpb = 2 if k % 2 == 0 else 4
                    with t.Fori(0, DOWN_GROUPS // gpb) as i:
                        for b in range(gpb):
                            group(n4 + i * (k * gpb // RING), b * k, k, g + i * gpb + b, b % 2,
                                  from_ffn(l * FF_PAIRS + pair0))
                    pair0 += FF_PART[part] // 2
                    n4 += DOWN_SLABS[part] // RING
                    g += DOWN_GROUPS
            mean_square(2 * DEPTH)


def constants():
    import numpy as np
    c = np.zeros((P, C_AT[-1]), np.float32)

    def at(i):
        return c[:, C_AT[i]:C_AT[i + 1]]
    half = ROT_DIM // 2
    pos = np.concatenate([np.arange(SEQ), np.tile(PAST_LEN + np.arange(DEC_SEQ), DEC_BATCH)]).astype(np.float32)
    inv = np.float32(ROPE_THETA) ** (-np.arange(half, dtype=np.float32) * np.float32(2.0) / np.float32(ROT_DIM))
    ang = (pos[None, :] * inv.astype(np.float32)[:, None]).astype(np.float32)
    at(C_COS)[:] = 1.0
    for head in (0, HEAD_DIM):
        for part in (0, half):
            at(C_COS)[head + part:head + part + half] = np.cos(ang)
            at(C_SIN)[head + part:head + part + half] = np.sin(ang)
        for d in range(half):
            at(C_ROT)[head + half + d, head + d] = -1.0
            at(C_ROT)[head + d, head + half + d] = 1.0
    at(C_ID)[:] = np.eye(P)
    i = np.arange(P)
    own = np.where(i[None, :] <= i[:, None], 0.0, NEG_BIG)
    prev = np.where(i[None, :] >= i[:, None], 0.0, NEG_BIG)
    at(C_MASKP)[:] = np.concatenate([own, prev, own], axis=1)
    at(C_HM)[:] = (i[:, None] // SUB == i[None, :] // SUB) & (i[:, None] <= i[None, :])
    tok = i % DEC_SEQ
    at(C_MC)[:] = np.where(i[None, :] >= tok[:, None], 0.0, NEG_BIG)
    j = np.arange(SAMP)
    at(C_MN)[:] = np.where((j[None, :] // DEC_SEQ == i[:, None] // (4 * DEC_SEQ)) &
                           (j[None, :] % DEC_SEQ <= tok[:, None]), 0.0, NEG_BIG)
    at(C_SM)[0:SAMP] = (j[:, None] // DEC_SEQ == j[None, :] // DEC_SEQ) & (j[:, None] <= j[None, :])
    at(C_VM)[0:SAMP] = j[:, None] // DEC_SEQ == np.arange(DEC_BATCH)[None, :]
    return c


def weight_stream(w_in, w_out, w_gate_up, w_down):
    import numpy as np
    n = SLAB_K * P

    def slabs(w, out):
        v = w.reshape(w.shape[0] // n, SLAB_K, P, w.shape[1] // SLAB_N, SLAB_N).transpose(3, 0, 2, 1, 4)
        out[:] = v.reshape(out.shape)

    stream = np.empty((DEPTH * SLABS, P, SLAB_K * SLAB_N), np.float32)
    for l in range(DEPTH):
        at = l * SLABS

        def take(k):
            nonlocal at
            at += k
            return stream[at - k:at]
        qkv, hgrn = (CB - Q0) * P, Q0 * P
        slabs(w_in[l][:, qkv:qkv + hgrn], take(hgrn // SLAB_N * (KC // SLAB_K)))
        slabs(w_in[l][:, :qkv], take(qkv // SLAB_N * (KC // SLAB_K)))
        slabs(w_in[l][:, qkv + hgrn:], take((IN_TILES - CB) // 2 * (KC // SLAB_K)))
        rows = w_out[l].reshape(4, D_MODEL // 4, D_MODEL)
        slabs(rows[[2, 0]].reshape(D_MODEL // 2, D_MODEL), take(OUT_SLABS))
        slabs(rows[[3, 1]].reshape(D_MODEL // 2, D_MODEL), take(OUT_SLABS))
        f0 = 0
        for part in range(2):
            f1 = f0 + FF_PART[part] * P
            up = take(UP_SLABS[part]).reshape(FF_PART[part] // 2, 2, KC // SLAB_K, P, SLAB_K * SLAB_N)
            for side in range(2):
                slabs(w_gate_up[l][:, side * D_FF + f0:side * D_FF + f1], up[:, side])
            slabs(w_down[l][f0:f1], take(DOWN_SLABS[part]))
            f0 = f1
    return stream


def kernel(**inputs):
    import numpy as np
    import concourse.bacc as bacc
    from concourse.bass_utils import run_bass_kernel_spmd

    a = {k: np.asarray(v) for k, v in inputs.items()}

    def chunks(v):
        return v.reshape(-1, P).T

    tokens = np.concatenate([a["x_prompt"].reshape(SEQ, D_MODEL), a["x_sample"].reshape(SAMP, D_MODEL)])
    gains = [g for l in range(DEPTH) for g in (a["norm_mix"][l], a["norm_ffn"][l])] + [a["norm_final"]]
    sink = a["attn_sink"]
    rows = np.broadcast_to(sink.reshape(DEPTH, 1, N_KV, 4, 1), (DEPTH, DEC_BATCH, N_KV, 4, DEC_SEQ))
    params = np.concatenate([
        chunks(np.concatenate(gains)), chunks(a["hgrn_lower_bounds"]), chunks(a["hgrn_norm"]), chunks(a["conv_w"]),
        np.broadcast_to(sink.reshape(1, -1), (P, DEPTH * N_Q)),
        rows.transpose(1, 3, 4, 0, 2).reshape(P, DEPTH * N_KV)], axis=1)
    kv = [a[n].reshape(DEPTH, DEC_BATCH, WINDOW, 2, P) for n in ("cache_attn_k", "cache_attn_v")]
    ins = {
        "wstream": weight_stream(a["w_in"], a["w_out"], a["w_gate_up"], a["w_down"]),
        "x_in": tokens.reshape(TOK, KC, P).transpose(2, 1, 0),
        "consts": constants(),
        "params": params,
        "conv_buf": a["state_conv"].reshape(DEPTH, 2 * DEC_BATCH, 4, P).transpose(0, 3, 2, 1),
        "kt_cache": kv[0].transpose(0, 3, 4, 1, 2).reshape(DEPTH * 2, P, DEC_BATCH, WINDOW),
        "v_cache": kv[1].transpose(0, 3, 2, 1, 4).reshape(DEPTH * 2, WINDOW, DEC_BATCH, P),
        "caches": np.stack(kv).reshape(2 * DEPTH * DEC_BATCH, WINDOW, 2 * P),
        "s_cache": a["state_hgrn"].transpose(0, 2, 3, 1, 4).reshape(DEPTH * HG_HEADS, P, DEC_BATCH, P),
    }
    outs = {
        "y_out": (P, KC, TOK),
        "kp_out": (DEPTH * 2, P, WINDOW), "vp_out": (DEPTH * 2, P, WINDOW),
        "ks_out": (DEPTH * 2, P, SAMP), "vs_out": (DEPTH * 2, P, SAMP),
        "caches_out": (2 * DEPTH * DEC_BATCH, WINDOW - DEC_SEQ, 2 * P),
        "hp_out": (DEPTH * HG_HEADS, P, P), "hs_out": (DEPTH * HG_HEADS, P, DEC_BATCH, P),
        "cv_out": (DEPTH, P, 4, 18),
    }
    nc = bacc.Bacc("TRN2", target_bir_lowering=False, num_devices=1)
    ins = {k: np.ascontiguousarray(v) for k, v in ins.items()}
    aps = [nc.dram_tensor(k, v.shape, F32, kind="ExternalInput").ap() for k, v in ins.items()]
    aps += [nc.dram_tensor(k, s, F32, kind="ExternalOutput").ap() for k, s in outs.items()]
    build(nc, *aps)
    r = run_bass_kernel_spmd(nc, [ins], core_ids=[0]).results[0]

    y = r["y_out"].transpose(2, 1, 0).reshape(TOK, D_MODEL)
    moved = r["caches_out"].reshape(2, DEPTH, DEC_BATCH, WINDOW - DEC_SEQ, N_KV, HEAD_DIM)

    def prompt_kv(v):
        return v.reshape(DEPTH, N_KV, HEAD_DIM, WINDOW).transpose(0, 3, 1, 2).reshape(DEPTH, 1, WINDOW, N_KV, HEAD_DIM)

    def sample_kv(v, old):
        new = v.reshape(DEPTH, N_KV, HEAD_DIM, DEC_BATCH, DEC_SEQ).transpose(0, 3, 4, 1, 2)
        return np.concatenate([old, new], axis=2)

    cv = r["cv_out"].transpose(0, 3, 2, 1).reshape(DEPTH, 18, 4 * P)
    return (y[:SEQ].reshape(1, SEQ, D_MODEL), y[SEQ:].reshape(DEC_BATCH, DEC_SEQ, D_MODEL),
            prompt_kv(r["kp_out"]), prompt_kv(r["vp_out"]),
            r["hp_out"].reshape(DEPTH, 1, HG_HEADS, P, P),
            np.ascontiguousarray(cv[:, :2]).reshape(DEPTH, 1, 2, 4 * P),
            sample_kv(r["ks_out"], moved[0]), sample_kv(r["vs_out"], moved[1]),
            r["hs_out"].reshape(DEPTH, HG_HEADS, P, DEC_BATCH, P).transpose(0, 3, 1, 2, 4),
            np.ascontiguousarray(cv[:, 2:]).reshape(DEPTH, DEC_BATCH, 2, 4 * P))
```
